# Optimizing a Trainium2 kernel written in Bass

```python
import jax
import jax.numpy as jnp
from jax import lax
import numpy as np

D_MODEL = 1024
BATCH = 1
SEQ = 256
DEPTH = 2
DEC_BATCH = 8
DEC_SEQ = 1
PAST_LEN = 2048
PAGE_SIZE = 128

HEAD_SIZE = 64
N_HEADS = D_MODEL // HEAD_SIZE
DECAY_LORA = 64
AAA_LORA = 64
GATE_LORA = 128
CONV_WIDTH = 31
D_FF = ((8 * D_MODEL // 3 + 127) // 128) * 128
N_EXPERTS = 8
TOP_K = 2
D_FF_EXPERT = D_FF // 2
N_RWKV = (DEPTH + 1) // 2
N_CONV = DEPTH // 2
RMS_EPS = 1e-6
LN_EPS = 1e-5
GN_EPS = 64e-5

kernel_name = "rwkv7_conformer_conv_hybrid_adaln_step"

def rms_norm(x, g):
    xf = x.astype(jnp.float32)
    y = xf * lax.rsqrt(jnp.mean(xf * xf, axis=-1, keepdims=True) + RMS_EPS)
    return (y * g.astype(jnp.float32)).astype(x.dtype)

def adaln(c, w, b, n):
    p = jax.nn.silu(c) @ w + b
    return jnp.split(p, n, axis=-1)

def modulate(h, shift, scale):
    return h * (1 + scale[:, None, :]) + shift[:, None, :]

def rwkv7_time_mix(h, shift_prev, s0, mu, w_r, w_k, w_v, w_o, w0, w1, w2, a0, a1, a2,
                   g1, g2, k_k, k_a, r_k, lnx_g, lnx_b):
    B, T, D = h.shape
    f32 = jnp.float32
    h_prev = jnp.concatenate([shift_prev[:, None, :].astype(h.dtype), h[:, :-1]], axis=1)
    xx = h_prev - h
    xr, xw, xk, xv, xa, xg = [h + xx * mu[i] for i in range(6)]
    r = xr @ w_r
    k = xk @ w_k
    v = xv @ w_v
    w_raw = (w0 + jnp.tanh(xw @ w1) @ w2).astype(f32)
    log_decay = -jnp.exp(-jax.nn.softplus(-w_raw) - 0.5)
    a = jax.nn.sigmoid((a0 + (xa @ a1) @ a2).astype(f32))
    g = jax.nn.sigmoid(xg @ g1) @ g2

    def heads(t):
        return t.astype(f32).reshape(B, T, N_HEADS, HEAD_SIZE)

    kk = heads(k * k_k)
    kk = kk / jnp.maximum(jnp.sqrt(jnp.sum(kk * kk, axis=-1, keepdims=True)), 1e-12)
    k_eff = k.astype(f32) * (1 + (a - 1) * k_a.astype(f32))
    rh, kh, vh, ah = heads(r), heads(k_eff), heads(v), heads(a)
    decay = jnp.exp(heads(log_decay))

    def tm(t):
        return jnp.swapaxes(t, 0, 1)

    def step(S, inp):
        r_t, w_t, k_t, v_t, a_t, b_t = inp
        sa = jnp.einsum('bhij,bhj->bhi', S, a_t)
        S = S * w_t[:, :, None, :] + sa[..., None] * b_t[:, :, None, :] + v_t[..., None] * k_t[:, :, None, :]
        y = jnp.einsum('bhij,bhj->bhi', S, r_t)
        return S, y

    s_final, ys = lax.scan(step, s0.astype(f32),
                           (tm(rh), tm(decay), tm(kh), tm(vh), tm(-kk), tm(kk * ah)))
    y = jnp.swapaxes(ys, 0, 1)
    mean = jnp.mean(y, axis=-1, keepdims=True)
    var = jnp.mean(jnp.square(y - mean), axis=-1, keepdims=True)
    yn = ((y - mean) * lax.rsqrt(var + GN_EPS)).reshape(B, T, D) * lnx_g.astype(f32) + lnx_b.astype(f32)
    bonus = (jnp.sum(rh * kh * r_k.astype(f32), axis=-1, keepdims=True) * vh).reshape(B, T, D)
    out = ((yn + bonus).astype(h.dtype) * g) @ w_o
    return out, h[:, -1], s_final.astype(h.dtype)

def conformer_conv(h, buf, pw1_w, pw1_b, dw_w, dw_b, ln_g, ln_b, pw2_w, pw2_b):
    D = h.shape[-1]
    u = h @ pw1_w + pw1_b
    u = u[..., :D] * jax.nn.sigmoid(u[..., D:])
    full = jnp.concatenate([buf.astype(u.dtype), u], axis=1)
    z = lax.conv_general_dilated(full, dw_w[:, None, :].astype(u.dtype), window_strides=(1,),
                                 padding='VALID', dimension_numbers=('NWC', 'WIO', 'NWC'),
                                 feature_group_count=D) + dw_b
    zf = z.astype(jnp.float32)
    mean = jnp.mean(zf, axis=-1, keepdims=True)
    var = jnp.mean(jnp.square(zf - mean), axis=-1, keepdims=True)
    zn = ((zf - mean) * lax.rsqrt(var + LN_EPS) * ln_g.astype(jnp.float32) + ln_b.astype(jnp.float32)).astype(h.dtype)
    out = jax.nn.silu(zn) @ pw2_w + pw2_b
    return out, full[:, -(CONV_WIDTH - 1):, :]

def swiglu(h, w1, w3, w2):
    return (jax.nn.silu(h @ w1) * (h @ w3)) @ w2

def moe_swiglu(h, router_w, router_b, w1, w3, w2):
    logits = (h @ router_w + router_b).astype(jnp.float32)
    top_v, top_i = lax.top_k(logits, TOP_K)
    gates = jax.nn.softmax(top_v, axis=-1)
    combine = jnp.sum(jax.nn.one_hot(top_i, N_EXPERTS, dtype=jnp.float32) * gates[..., None], axis=-2)
    y = jnp.zeros_like(h)
    for e in range(N_EXPERTS):
        y = y + combine[..., e:e + 1].astype(h.dtype) * swiglu(h, w1[e], w3[e], w2[e])
    return y

def run_trunk(x, c, wkv0, shift0, conv0, shared, rw, cv, ffn, moe, fin):
    ada_w, ada_b, norm_mix_g, norm_ffn_g = shared
    wkv_out, shift_out, conv_out = [], [], []
    for i in range(DEPTH):
        j = i // 2
        sh1, sc1, gt1, sh2, sc2, gt2 = adaln(c, ada_w[i], ada_b[i], 6)
        h = modulate(rms_norm(x, norm_mix_g[i]), sh1, sc1)
        if i % 2 == 0:
            o, last, s = rwkv7_time_mix(h, shift0[j], wkv0[j], *[p[j] for p in rw])
            shift_out.append(last)
            wkv_out.append(s)
        else:
            o, buf = conformer_conv(h, conv0[j], *[p[j] for p in cv])
            conv_out.append(buf)
        x = x + gt1[:, None, :] * o
        h = modulate(rms_norm(x, norm_ffn_g[i]), sh2, sc2)
        if i % 2 == 0:
            f = swiglu(h, *[p[j] for p in ffn])
        else:
            f = moe_swiglu(h, *[p[j] for p in moe])
        x = x + gt2[:, None, :] * f
    final_g, final_ada_w, final_ada_b = fin
    sh, sc = adaln(c, final_ada_w, final_ada_b, 2)
    y = modulate(rms_norm(x, final_g), sh, sc)
    return y, jnp.stack(wkv_out), jnp.stack(shift_out), jnp.stack(conv_out)

def setup_inputs(seed: int = 0) -> dict:
    key = jax.random.key(seed)
    keys = jax.random.split(key, 64)
    cnt = [0]

    def nxt():
        cnt[0] += 1
        return keys[cnt[0] - 1]

    def nrm(shape, scale):
        return jax.random.normal(nxt(), shape, jnp.float32) * scale

    def unif(shape, lo, hi):
        return jax.random.uniform(nxt(), shape, jnp.float32, lo, hi)

    D = D_MODEL
    dinv = D ** -0.5
    A, C = N_RWKV, N_CONV
    inp = {}
    inp['x_prompt'] = nrm((BATCH, SEQ, D), 1.0)
    inp['x_sample'] = nrm((DEC_BATCH, DEC_SEQ, D), 1.0)
    inp['state_wkv'] = nrm((A, DEC_BATCH, N_HEADS, HEAD_SIZE, HEAD_SIZE), 0.3)
    inp['state_shift'] = nrm((A, DEC_BATCH, D), 1.0)
    inp['state_conv'] = nrm((C, DEC_BATCH, CONV_WIDTH - 1, D), 0.5)
    inp['c_prompt'] = nrm((BATCH, D), 1.0)
    inp['c_sample'] = nrm((DEC_BATCH, D), 1.0)
    inp['ada_w'] = nrm((DEPTH, D, 6 * D), 0.5 * dinv)
    inp['ada_b'] = nrm((DEPTH, 6 * D), 0.02)
    inp['norm_mix_g'] = 1.0 + nrm((DEPTH, D), 0.05)
    inp['norm_ffn_g'] = 1.0 + nrm((DEPTH, D), 0.05)
    inp['rw_mu'] = unif((A, 6, D), 0.0, 1.0)
    inp['rw_wr'] = nrm((A, D, D), dinv)
    inp['rw_wk'] = nrm((A, D, D), dinv)
    inp['rw_wv'] = nrm((A, D, D), dinv)
    inp['rw_wo'] = nrm((A, D, D), dinv)
    inp['rw_w0'] = unif((A, D), -5.5, -0.5)
    inp['rw_w1'] = nrm((A, D, DECAY_LORA), dinv)
    inp['rw_w2'] = nrm((A, DECAY_LORA, D), 0.1)
    inp['rw_a0'] = nrm((A, D), 0.1)
    inp['rw_a1'] = nrm((A, D, AAA_LORA), dinv)
    inp['rw_a2'] = nrm((A, AAA_LORA, D), 0.5 * AAA_LORA ** -0.5)
    inp['rw_g1'] = nrm((A, D, GATE_LORA), dinv)
    inp['rw_g2'] = nrm((A, GATE_LORA, D), GATE_LORA ** -0.5)
    inp['rw_kk'] = 0.85 + nrm((A, D), 0.05)
    inp['rw_ka'] = 1.0 + nrm((A, D), 0.05)
    inp['rw_rk'] = nrm((A, N_HEADS, HEAD_SIZE), 0.1)
    inp['rw_lnx_g'] = 1.0 + nrm((A, D), 0.05)
    inp['rw_lnx_b'] = nrm((A, D), 0.01)
    inp['cv_pw1_w'] = nrm((C, D, 2 * D), dinv)
    inp['cv_pw1_b'] = nrm((C, 2 * D), 0.01)
    inp['cv_dw_w'] = nrm((C, CONV_WIDTH, D), CONV_WIDTH ** -0.5)
    inp['cv_dw_b'] = nrm((C, D), 0.01)
    inp['cv_ln_g'] = 1.0 + nrm((C, D), 0.05)
    inp['cv_ln_b'] = nrm((C, D), 0.01)
    inp['cv_pw2_w'] = nrm((C, D, D), dinv)
    inp['cv_pw2_b'] = nrm((C, D), 0.01)
    inp['ffn_w1'] = nrm((A, D, D_FF), dinv)
    inp['ffn_w3'] = nrm((A, D, D_FF), dinv)
    inp['ffn_w2'] = nrm((A, D_FF, D), D_FF ** -0.5)
    inp['moe_router_w'] = nrm((C, D, N_EXPERTS), dinv)
    inp['moe_router_b'] = nrm((C, N_EXPERTS), 0.01)
    inp['moe_w1'] = nrm((C, N_EXPERTS, D, D_FF_EXPERT), dinv)
    inp['moe_w3'] = nrm((C, N_EXPERTS, D, D_FF_EXPERT), dinv)
    inp['moe_w2'] = nrm((C, N_EXPERTS, D_FF_EXPERT, D), D_FF_EXPERT ** -0.5)
    inp['final_g'] = 1.0 + nrm((D,), 0.05)
    inp['final_ada_w'] = nrm((D, 2 * D), 0.5 * dinv)
    inp['final_ada_b'] = nrm((2 * D,), 0.02)
    return inp

def reference(x_prompt, x_sample, state_wkv, state_shift, state_conv, c_prompt, c_sample,
              ada_w, ada_b, norm_mix_g, norm_ffn_g,
              rw_mu, rw_wr, rw_wk, rw_wv, rw_wo, rw_w0, rw_w1, rw_w2, rw_a0, rw_a1, rw_a2,
              rw_g1, rw_g2, rw_kk, rw_ka, rw_rk, rw_lnx_g, rw_lnx_b,
              cv_pw1_w, cv_pw1_b, cv_dw_w, cv_dw_b, cv_ln_g, cv_ln_b, cv_pw2_w, cv_pw2_b,
              ffn_w1, ffn_w3, ffn_w2,
              moe_router_w, moe_router_b, moe_w1, moe_w3, moe_w2,
              final_g, final_ada_w, final_ada_b):
    shared = (ada_w, ada_b, norm_mix_g, norm_ffn_g)
    rw = (rw_mu, rw_wr, rw_wk, rw_wv, rw_wo, rw_w0, rw_w1, rw_w2, rw_a0, rw_a1, rw_a2,
          rw_g1, rw_g2, rw_kk, rw_ka, rw_rk, rw_lnx_g, rw_lnx_b)
    cv = (cv_pw1_w, cv_pw1_b, cv_dw_w, cv_dw_b, cv_ln_g, cv_ln_b, cv_pw2_w, cv_pw2_b)
    ffn = (ffn_w1, ffn_w3, ffn_w2)
    moe = (moe_router_w, moe_router_b, moe_w1, moe_w3, moe_w2)
    fin = (final_g, final_ada_w, final_ada_b)
    b = x_prompt.shape[0]
    dt = x_prompt.dtype
    zero_wkv = jnp.zeros((N_RWKV, b, N_HEADS, HEAD_SIZE, HEAD_SIZE), dt)
    zero_shift = jnp.zeros((N_RWKV, b, D_MODEL), dt)
    zero_conv = jnp.zeros((N_CONV, b, CONV_WIDTH - 1, D_MODEL), dt)
    y_prompt, wkv_prompt, shift_prompt, conv_prompt = run_trunk(
        x_prompt, c_prompt, zero_wkv, zero_shift, zero_conv, shared, rw, cv, ffn, moe, fin)
    y_sample, wkv_sample, shift_sample, conv_sample = run_trunk(
        x_sample, c_sample, state_wkv, state_shift, state_conv, shared, rw, cv, ffn, moe, fin)
    return (y_prompt, y_sample, wkv_prompt, shift_prompt, conv_prompt, wkv_sample, shift_sample, conv_sample)


_drawn_inputs = setup_inputs


def setup_inputs(seed=0):
    import zlib

    import numpy as np

    out = dict(_drawn_inputs(seed))
    spreads = {}
    factors = {'rw_lnx_g': 5.383,
     'rw_lnx_b': 23.898,
     'cv_pw1_b': 5.704,
     'cv_dw_b': 8.0,
     'cv_ln_g': 3.858,
     'cv_ln_b': 36.889,
     'cv_pw2_b': 26.127,
     'moe_router_b': 14.717,
     'norm_ffn_g': 2.705}
    for name, (base, spread) in spreads.items():
        noise = np.random.default_rng([zlib.crc32(name.encode()), seed]).standard_normal(out[name].shape)
        drawn = base * np.exp(spread * noise) if base else spread * noise
        out[name] = jnp.asarray(drawn.astype(out[name].dtype))
    for name, factor in factors.items():
        out[name] = (out[name] * factor).astype(out[name].dtype)
    return out
```

```python
from contextlib import ExitStack

import concourse.bass as bass
from concourse import mybir

F32 = mybir.dt.float32
I32 = mybir.dt.int32
ALU = mybir.AluOpType
ACT = mybir.ActivationFunctionType
AX = mybir.AxisListType.X

D = 1024
NB = D // 128
SEQ = 256
NS = 8
T = SEQ + NS
NC = 1 + NS
C = 64
NCH = SEQ // C
CW = 31
TAPS = 15
NV = 6
NF = 22
NE = 8
FE = 11
CAP = 96
NJ = NE + (2 * T) // CAP
BIG = 4096.0
RMS_EPS, LN_EPS, GN_EPS = 1e-6, 1e-5, 64e-5
DECAY = -0.6065306597126334

PCOL, _n = {}, 0
for _name, _w in (("ada_b", 112), ("norm_mix_g", 16), ("norm_ffn_g", 16), ("mu", 48), ("w0", 8), ("a0", 8),
                  ("kk", 8), ("ka", 8), ("rk", 8), ("lnx_g", 8), ("lnx_b", 8), ("pw1_b", 16), ("dw_b", 8),
                  ("ln_g", 8), ("ln_b", 8), ("pw2_b", 8), ("final_g", 8), ("dw", NB * CW)):
    PCOL[_name] = _n
    _n += _w
NPAR = _n

SLOT = 2048
MSLOT = 3 * D


def plan_stream():
    plan = []
    for n, key in enumerate([("ada", n) for n in range(24)] + [("rkv", n) for n in range(12)]
                            + [("ada", n) for n in range(24, 56)] + [("g2", 0)] + [("wo", n) for n in range(4)]):
        plan.append((key, D if key[0] == "g2" else SLOT, n % 4))
    first = len(plan)
    order = list(range(4, 12)) + list(range(4))
    then = [("up", n) for n in range(NF)] + [("down", n) for n in range(2 * NB)]
    for n, key in enumerate(then):
        plan.append((key, FE * 128 if key[0] == "down" else SLOT, order[n % 12]))
    late = [s for s in (order[(len(then) + n) % 12] for n in range(12)) if s < 8]
    plan += [(("pw1", n), SLOT, late[n]) for n in range(8)]
    plan += [(("pw2", n), SLOT, 8 + n) for n in range(4)]
    return plan, first


def build(nc, io):
    ctx = ExitStack()
    with ctx:
        arena = ctx.enter_context(nc.sbuf_tensor("arena", [128, 53100], F32))
        top = [0]

        def at(off, *shape):
            n = 1
            for s in shape:
                n *= s
            v = arena[:, off:off + n]
            if len(shape) == 2:
                v = v.rearrange("p (a b) -> p a b", a=shape[0])
            if len(shape) == 3:
                v = v.rearrange("p (a b c) -> p a b c", a=shape[0], b=shape[1])
            return v

        def keep(*shape):
            n = 1
            for s in shape:
                n *= s
            v = at(top[0], *shape)
            top[0] += n
            return v

        x = keep(NB, T)
        h = keep(NB, T + 1)
        par = keep(NPAR)
        mod = keep(112, NC)
        ident = keep(128)
        ones = keep(128)
        bdones = keep(128)
        m_su = keep(128)
        m_iu = keep(C)
        m_p = keep(128)
        m_pt = keep(128)
        m_32t = keep(128)
        m_64t = keep(128)
        scanm = keep(T)
        scr = keep(NB, T)
        rstd = keep(T)
        rtmp = keep(T)
        gain = keep(NB, NC)
        smt = keep(2, NB, NS)
        eps = keep(4)
        csil = keep(NB, NC)
        tg = keep(T)
        arow = keep(2, 512)
        id64 = keep(C)
        tri = keep(128)
        iota_c = keep(CAP)
        iota_e = keep(NE)
        eidx = keep(16)
        shb = keep(NB, NC)
        shf = keep(NB, NS)
        base = top[0]

        ring1 = [at(base + SLOT * n, SLOT) for n in range(4)]
        rw = base + 4 * SLOT
        rt, vt, att, btt, ktt = (at(rw + 2112 * n, NB, T) for n in range(5))
        ck = rw + 5 * 2112
        assert ck + 2112 * 3 >= base + 12 * SLOT
        xx = at(ck, NB, T)
        xi = [at(ck + 2112 * (1 + n), NB, T) for n in range(2)]
        lw = at(ck + 2112 * 3, NB, T)
        cum = at(ck + 2112 * 4, NB, T)
        ex = at(ck + 2112 * 5, NB, T)
        tmp = at(ck + 2112 * 6, NB, T)
        lo1 = at(ck + 2112 * 7, NB, 256)
        lo2 = at(ck + 2112 * 7 + 2048, D)
        bd = [at(ck + 1024 * n, NB, 128) for n in range(16)]
        (abd, bbd, kbd, vbd, btm, ktm, ntm, pt_, p_, m32, m64, tt_, uu_, ww_, sabd, s0bd) = bd
        st = [at(ck + 1024 * 16 + 512 * n, NB, C) for n in range(6)]
        (vst, qbt, qkt, xst, sast, s0st) = st
        sp0 = ck + 1024 * 19
        smp = at(sp0, 6 * NB, NS)
        sst = [at(sp0 + 384 + 512 * n, NS, C) for n in range(2)]
        sq1, sq2, sq3 = (at(sp0 + 384 + 1024 + 512 * n, NS, C) for n in range(3))
        ecl = at(sp0 + 384 + 2560, NB, NCH)
        ysm = at(sp0 + 384 + 2560 + 32, NB, NS)
        assert sp0 + 384 + 2560 + 32 + 64 <= 53100, sp0 + 3040
        yy = h[:, :, 1:T + 1]
        bonus = scr
        gg, oo, scr2 = (at(ck + 2112 * n, NB, T) for n in (3, 4, 5))
        gmean = at(ck + 2112 * 6, NB, T)
        ring2 = [at(base + SLOT * n, SLOT) for n in range(12)]
        r2e = base + 12 * SLOT
        ff = at(r2e, NF, T)
        cvb = r2e + NF * T
        upad = at(cvb, NB, SEQ + CW - 1)
        zz = at(cvb + NB * (SEQ + CW - 1), NB, T)
        cbuf = at(cvb + NB * (SEQ + CW - 1) + 2112, NB * NS, CW)
        cprd = at(cvb + NB * (SEQ + CW - 1) + 2112 + NB * NS * CW, NB * NS, CW)
        glf = at(cvb, 2, T)
        gl = at(r2e, 2, T)
        NDG = (NF * T - 2 * T) // 128
        diag = at(r2e + 2 * T, NDG, 128)
        ring3 = [at(base + MSLOT * n, MSLOT) for n in range(FE)]
        mo = base + FE * MSLOT
        htm = at(mo, 3, D)
        xe = h
        he = at(mo + 3072, FE, CAP)
        sel = at(mo + 3072 + 1056, 3, CAP)
        selg = at(mo + 3072 + 1056 + 288, 3, CAP)
        selt = at(mo + 3072 + 1056 + 576, T)
        yout = at(mo + 3072 + 1056 + 576 + 264, D)
        mt0 = mo + 3072 + 1056 + 576 + 264 + 1024
        lg = at(mt0, 3, NE)
        sc1 = at(mt0 + 24, 3, NE)
        sc2 = at(mt0 + 48, 3, NE)
        oh1 = at(mt0 + 72, 3, NE)
        oh2 = at(mt0 + 96, 3, NE)
        msk = at(mt0 + 120, 3, NE)
        jr = at(mt0 + 144, 3, NJ + 1)
        jg = at(mt0 + 144 + 42, 3, NJ + 1)
        cur = at(mt0 + 228, 6)
        cnt = at(mt0 + 340, NE)
        flg = at(mt0 + 348, 16)
        pos = at(mt0 + 364, 16)
        jm = at(mt0 + 380, 16)
        rx = at(mt0 + 412, 3, 16)
        gx = at(mt0 + 460, 3, 16)
        jt = at(mt0 + 508, 3, 16)
        jobf = at(mt0 + 556, 8)
        mx = at(mt0 + 564, 6)
        rwt = at(mt0 + 572, NB, NE)
        rbr = at(mt0 + 636, NE)
        silm = at(mt0 + 644, 2, CAP)
        assert mt0 + 644 + 192 <= 53100, mt0 + 964
        jobi = ctx.enter_context(nc.sbuf_tensor("jobi", [1, 8], I32))

        bank = [ctx.enter_context(nc.psum_tensor(f"bank{n}", [128, 512], F32)) for n in range(8)]
        SEMS = """consts c_in csil par_in x_in lora_in shift_in conv_in router_in
            ada_mm ada_row ada_tr ada_ev square norm_sum norm_root norm_rstd gain hmul hadd hsamp
            xx xi kk_sq kk_root rk_prod p1_ready expc chunk_d chunk_p zeros
            e_P e_T1 e_PT e_M32 e_M64 e_U1 e_NT e_QBT e_QKT e_T2 e_U2 e_T3 e_U3 e_T4 e_U4 e_T5 e_U5 e_U6
            e_P2 e_P2T e_P4 e_P4T e_P8 e_Btm e_Ktm e_Vtm e_Vst e_W e_W2 e_X e_SA e_SAbd e_Y e_S0
            s_in s_out s_terms s_read s_fold s_sq3
            gn_centered gn_square gn_root gn_out ff_up ff_sil ff_h x_new glu_gate glu_mm conv_done tap diag conv_mm conv_ev
            ln_mean ln_centered ln_square ln_root ln_scaled z_ready
            logits tokmajor tok_ev ranks_in ranked sel selg gath xe_ev w13 sil hev job y_ev sel_t selt_ev scat scat_ev
            curr curg x_job diff ediff joblist y_out shift_o wkv_o conv_o shb_ready
            dve_chain pool_chain act_chain""".split()
        sems = {name: ctx.enter_context(nc.semaphore(name)) for name in SEMS}
        S = sems.__getitem__
        slot_in = [ctx.enter_context(nc.semaphore(f"slot_in{n}")) for n in range(12)]
        mslot_in = [ctx.enter_context(nc.semaphore(f"mslot_in{n}")) for n in range(FE)]
        cfull = [ctx.enter_context(nc.semaphore(f"chunk_bank_full{n}")) for n in range(4)]
        pfull = [ctx.enter_context(nc.semaphore(f"out_bank_full{n}")) for n in range(2)]
        pfree = [ctx.enter_context(nc.semaphore(f"out_bank_free{n}")) for n in range(2)]

        def wait(eng, name, val):
            if not (isinstance(val, int) and val <= 0):
                eng.wait_ge(sems[name], val)

        plan, n_first = plan_stream()
        piece_of, occupant, used = {}, {}, [0] * 12
        before = []
        for key, w, s in plan:
            used[s] += 1
            before.append(occupant.get(s))
            occupant[s] = key
            ring = ring1 if len(before) <= n_first else ring2
            piece_of[key] = (ring[s][:, 0:w], s, 16 * used[s])

        def pc(name, b, n=1):
            o = PCOL[name] + b
            return par[:, o:o + n]

        PRODS = [("M", 2), ("MT", 2), ("P2", 2), ("P2T", 2), ("NT", 2), ("QBT", 1), ("QKT", 1), ("T2", 2), ("U2", 2),
                 ("P4", 2), ("P4T", 2), ("Btm", 2), ("Ktm", 2), ("Vtm", 2), ("T3", 2), ("U3", 2), ("P8", 2), ("T4", 2),
                 ("U4", 2), ("W", 2), ("T5", 2), ("U5", 2), ("W2", 2), ("U6", 2), ("X", 1), ("SA", 1), ("Y", 1), ("S", 1)]
        LAST = {"M": "P", "MT": "M64", "S": "S0"}
        GORD = [(c, nm, g, two) for c in range(NCH) for nm, two in PRODS for g in range(two)]
        GK = {(c, nm, g): k for k, (c, nm, g, two) in enumerate(GORD)}

        def gbank(c, nm, g):
            k = GK[c, nm, g]
            return bank[2 + k % 4], k % 4, k // 4 + 1

        def gfree(c, nm, g):
            k = GK[c, nm, g] - 4
            if k < 0:
                return None
            c, nm, g, two = GORD[k]
            nm = LAST.get(nm, nm)
            return "e_" + nm, (two * c + g + 1 if nm != "S0" else c + 2)

        STEPS = []
        for c in range(NCH):
            STEPS.append(("start", c))
            for nm, _ in PRODS:
                STEPS.append(("prod", c, nm))
                if nm in ("MT", "P8", "U4", "U5"):
                    STEPS.append(("ada",))
                if nm in ("P4T", "W"):
                    STEPS.append(("sample_a", 2 * c + (nm == "W")))
                if nm in ("T4", "W2"):
                    STEPS.append(("sample_b", 2 * c + (nm == "W2")))
        n_ada = 12
        for k, s in enumerate(STEPS):
            if s[0] == "ada":
                STEPS[k] = ("ada", n_ada)
                n_ada += 1
        STEPS += [("ada", n) for n in range(n_ada, 29)]

        PORD = []
        for nm, k in (("lw1", 1), ("la1", 1), ("lg1", 1), ("w", NB), ("a", NB), ("k", NB), ("kks", NB), ("r", NB),
                      ("bon", NB), ("v", NB), ("smp", 3 * NB), ("gnm", NB), ("gnv", NB), ("g2", NB), ("wo", NB),
                      ("up", NF), ("down", NB), ("pw1", NB), ("pw2", NB)):
            PORD += [(nm, n) for n in range(k)]
        PK = {key: k for k, key in enumerate(PORD)}

        def pbank(key):
            k = PK[key]
            return bank[k % 2], k % 2, k // 2 + 1

        def pwait_full(eng, key):
            eng.wait_ge(pfull[pbank(key)[1]], pbank(key)[2])

        def pwait_taken(eng, key):
            eng.wait_ge(pfree[pbank(key)[1]], pbank(key)[2])

        def consumed(eng, key):
            kind, n = key
            if kind == "ada":
                eng.wait_ge(S("ada_mm"), n + 1)
            elif kind == "rkv":
                pwait_full(eng, ("krv"[n // 4], 2 * (n % 4) + 1))
            elif kind in ("wo", "pw2"):
                pwait_full(eng, (kind, 2 * n + 1))
            elif kind == "g2":
                pwait_full(eng, ("g2", NB - 1))
            elif kind == "up":
                eng.wait_ge(S("ff_up"), n + 1)
            elif kind == "pw1":
                eng.wait_ge(S("glu_mm"), n + 1)
            elif kind == "down":
                pwait_full(eng, ("down", n // 2))

        DIAGS = sorted({CW * m for m in range(NB - NV)} | {q for q in range(NDG, CW * (NB - NV), NDG)})

        TOK = [(0, 128), (128, 256), (256, T)]
        block = ctx.enter_context(nc.Block())

        @block.sync
        def _(sp):
            sp.dma_start(csil[:, :, :], io["c"]).then_inc(S("c_in"), 16)
            for n, (key, w, s) in enumerate(plan):
                if before[n]:
                    consumed(sp, before[n])
                if n == n_first:
                    sp.wait_ge(cfull[gbank(NCH - 1, "S", 0)[1]], gbank(NCH - 1, "S", 0)[2])
                dst, _, _ = piece_of[key]
                src = io[key[0]] if key[0] == "g2" else io[key[0]][key[1]]
                sp.dma_start(dst, src).then_inc(slot_in[s], 16)
                if n == 1:
                    sp.dma_start(par, io["par"]).then_inc(S("par_in"), 16)
                    sp.dma_start(x[:, :, :], io["x"]).then_inc(S("x_in"), 16)
                    sp.dma_start(lo1[:, :, :], io["lo1"]).then_inc(S("lora_in"), 16)
                    sp.dma_start(lo2, io["lo2"]).then_inc(S("lora_in"), 16)
                    sp.dma_start(shf[:, :, :], io["shift"]).then_inc(S("shift_in"), 16)
                if key == ("up", 8):
                    pwait_taken(sp, ("wo", NB - 1))
                    sp.dma_start(cbuf[:, :, 0:CW - 1], io["conv"]).then_inc(S("conv_in"), 16)
            last = {s: key for key, w, s in plan}
            for f in range(FE):
                for s in range(12):
                    if s * SLOT < (f + 1) * MSLOT and f * MSLOT < (s + 1) * SLOT:
                        consumed(sp, last[s])
                if (f + 1) * MSLOT > 12 * SLOT:
                    pwait_full(sp, ("pw2", NB - 1))
                    sp.wait_ge(S("conv_o"), 32)
                sp.dma_start(ring3[f], io["moe"][f]).then_inc(mslot_in[f], 16)
            sp.dma_start(rwt[:, :, :], io["rw"]).then_inc(S("router_in"), 16)
            sp.dma_start(rbr[0:1, :], io["rb"]).then_inc(S("router_in"), 16)

            def stream(expert, j):
                for f in range(FE):
                    sp.wait_ge(S("job"), (j - 1) * FE + f + 1)
                    sp.dma_start(ring3[f], io["moe"][bass.ds(expert * FE + f, 1), :, :]
                                 .rearrange("a p n -> (a p) n")).then_inc(mslot_in[f], 16)

            with sp.Fori(1, NE) as j:
                stream(j, j)
            sp.wait_ge(S("joblist"), 1)
            extra = sp.value_load(jobi[0:1, 0:1], min_val=0, max_val=NJ - NE)
            with sp.If(extra > 0):
                with sp.Fori(0, extra) as m:
                    expert = sp.value_load(jobi[0:1, bass.ds(m + 1, 1)], min_val=0, max_val=NE - 1)
                    stream(expert, m + NE)
            for n in range(NB):
                sp.wait_ge(S("hadd"), 4 * NB + n + 1)
                sp.wait_ge(S("hsamp"), 5)
                sp.dma_start(io["y"][:, n, :], scr[:, n, :]).then_inc(S("y_out"), 16)
            sp.wait_ge(S("y_out"), 16 * NB)
            sp.wait_ge(S("shift_o"), 16)
            sp.wait_ge(S("wkv_o"), 16)
            sp.wait_ge(S("s_out"), 16 * NB)
            sp.wait_ge(S("conv_o"), 32)

        @block.tensor
        def _(pe):
            def arrived(key):
                dst, s, v = piece_of[key]
                pe.wait_ge(slot_in[s], v)
                return dst

            def pstart(key):
                b, i, u = pbank(key)
                if u > 1:
                    pe.wait_ge(pfree[i], u - 1)
                return b

            def pdone(key, ins):
                ins.then_inc(pfull[pbank(key)[1]], 1)

            def ada(n):
                if n < 28:
                    wait(pe, "ada_row", n)
                    for kh in range(2):
                        w = arrived(("ada", 2 * n + kh)).rearrange("p (k c) -> p k c", k=4)
                        for kb in range(4):
                            k = 4 * kh + kb
                            ins = pe.matmul(bank[6][0:NC, :], csil[:, k, :], w[:, kb, :], start=(k == 0),
                                            stop=(k == NB - 1))
                        ins.then_inc(S("ada_mm"), 1)
                if n and n != 12:
                    m = n - 1
                    pe.wait_ge(S("ada_row"), m + 1)
                    wait(pe, "ada_ev", m)
                    for j in range(4):
                        o = (m % 2) * 4 * NC + j * NC
                        ins = pe.transpose(bank[7][:, o:o + NC], arow[0:NC, m % 2, j * 128:(j + 1) * 128],
                                           ident[0:NC, 0:NC])
                    ins.then_inc(S("ada_tr"), 1)

            sums = [0]

            def channel_sum(src):
                for k in range(NB):
                    ins = pe.matmul(bank[7][:, 128:128 + T], ones, src[:, k, :], start=(k == 0), stop=(k == NB - 1))
                ins.then_inc(S("norm_sum"), 1)

            def dense(nm, keyf, rhs):
                for n in range(NB):
                    b = pstart((nm, n))
                    w = arrived(keyf(n // 2)).rearrange("p (o k c) -> p o k c", o=2, k=NB)
                    for k in range(NB):
                        ins = pe.matmul(b[:, 0:T], w[:, n % 2, k, :], rhs(k), start=(k == 0), stop=(k == NB - 1))
                    pdone((nm, n), ins)

            def heads_sum(nm, src):
                for n in range(NB):
                    b = pstart((nm, n))
                    pdone((nm, n), pe.matmul(b[:, 0:T], bdones, src[:, n, :], start=True, stop=True))

            pe.wait_ge(S("consts"), 1)
            pe.wait_ge(S("csil"), 1)
            for n in range(12):
                ada(n)
            pe.wait_ge(S("ada_row"), 12)
            pe.wait_ge(S("ada_ev"), 11)
            for j in range(4):
                o = 4 * NC + j * NC
                ins = pe.transpose(bank[7][:, o:o + NC], arow[0:NC, 1, j * 128:(j + 1) * 128], ident[0:NC, 0:NC])
            ins.then_inc(S("ada_tr"), 1)
            pe.wait_ge(S("square"), 1)
            pe.wait_ge(S("ada_ev"), 12)
            channel_sum(scr)

            pe.wait_ge(S("lora_in"), 32)
            for q, (nm, lo, hi) in enumerate((("lw1", 0, 64), ("la1", 64, 128), ("lg1", 128, 256))):
                b = pstart((nm, 0))
                pe.wait_ge(S("xi"), q + 1)
                o = b[64:128, 0:T] if nm == "la1" else b[0:hi - lo, 0:T]
                for k in range(NB):
                    ins = pe.matmul(o, lo1[:, k, lo:hi], xi[q % 2][:, k, :], start=(k == 0), stop=(k == NB - 1))
                pdone((nm, 0), ins)
            for q, nm in enumerate("wa"):
                pwait_taken(pe, (("lw1", 0), ("la1", 0))[q])
                for n in range(NB):
                    b = pstart((nm, n))
                    pdone((nm, n), pe.matmul(b[:, 0:T], lo2[64 * q:64 * q + 64, n * 128:(n + 1) * 128],
                                             ex[64 * q:64 * q + 64, 0, :], start=True, stop=True))
            pe.wait_ge(S("xi"), 4)
            dense("k", lambda m: ("rkv", m), lambda k: xi[1][:, k, :])
            pe.wait_ge(S("kk_sq"), 1)
            heads_sum("kks", scr)
            pe.wait_ge(S("xi"), 5)
            dense("r", lambda m: ("rkv", 4 + m), lambda k: xi[0][:, k, :])
            pe.wait_ge(S("rk_prod"), 1)
            heads_sum("bon", tmp)
            pe.wait_ge(S("xi"), 6)
            dense("v", lambda m: ("rkv", 8 + m), lambda k: xi[1][:, k, :])

            NEED = {
                "P2": ("PT", "P"), "P2T": ("PT", "P"), "T2": ("U1", "P2"), "U2": ("U1", "P2"), "P4": ("P2", "P2T"),
                "P4T": ("P2", "P2T"), "T3": ("U2", "P4"), "U3": ("U2", "P4"), "P8": ("P4", "P4T"),
                "T4": ("U3", "P8"), "U4": ("U3", "P8"), "W": ("M32", "T4"), "T5": ("U4", "W"), "U5": ("U4", "W"),
                "W2": ("M64", "T5"), "U6": ("U5", "W2"), "X": ("NT", "S0", "Vst"), "SA": ("U6", "X"),
                "Y": ("SAbd", "QBT", "QKT", "Vtm"), "S": ("Btm", "Ktm", "SA", "Vst")}
            WIDE = {nm for nm, two in PRODS if two == 2} | {"P", "PT", "M32", "M64", "U1", "T1"}
            TILES = {
                "M": [(abd, bbd)], "MT": [(bbd, abd)], "P2": [(pt_, p_)], "P2T": [(p_, pt_)], "NT": [(kbd, abd)],
                "QBT": [(bbd, None)], "QKT": [(kbd, None)], "T2": [(uu_, sabd)], "U2": [(sabd, uu_)],
                "P4": [(vbd, sabd)], "P4T": [(sabd, vbd)], "T3": [(uu_, p_)], "U3": [(p_, uu_)],
                "P8": [(pt_, p_)], "T4": [(uu_, sabd)], "U4": [(sabd, uu_)], "W": [(m32, tt_)], "T5": [(uu_, ww_)],
                "U5": [(ww_, uu_)], "W2": [(m64, tt_)], "U6": [(ww_, uu_)], "X": [(abd, s0st), (ntm, vst)],
                "SA": [(uu_, xst)], "Y": [(s0bd, None), (sabd, qbt), (vbd, qkt)],
                "S": [(btm, sast), (ktm, vst)]}
            TURN = {"Btm": bbd, "Ktm": kbd, "Vtm": ww_}

            def prod(c, nm):
                two = dict(PRODS)[nm]
                per = 8 // two
                width = 64 * two
                for g in range(two):
                    b, i, u = gbank(c, nm, g)
                    fr = gfree(c, nm, g)
                    if fr:
                        pe.wait_ge(S(fr[0]), fr[1])
                    for o_ in NEED.get(nm, ()):
                        if o_ in WIDE:
                            pe.wait_ge(S("e_" + o_), 2 * c + (g + 1 if two == 2 else 2))
                        else:
                            pe.wait_ge(S("e_" + o_), c + 1)
                    for q in range(per):
                        hp = per * g + q
                        o = b[:, q * width:(q + 1) * width]
                        if nm in TURN:
                            ins = pe.transpose(o, TURN[nm][:, hp, :], ident)
                            continue
                        for z, (l, r) in enumerate(TILES[nm]):
                            r = rt[:, hp, C * c:C * c + C] if r is None else r[:, hp, :]
                            ins = pe.matmul(o, l[:, hp, :], r, start=(z == 0), stop=(z == len(TILES[nm]) - 1))
                    ins.then_inc(cfull[i], 1)

            for step in STEPS:
                if step[0] == "start":
                    pe.wait_ge(S("chunk_d"), step[1] + 1)
                    pe.wait_ge(S("chunk_p"), step[1] + 1)
                elif step[0] == "prod":
                    prod(step[1], step[2])
                elif step[0] == "ada":
                    ada(step[1])
                elif step[0] == "sample_a":
                    hp = step[1]
                    for z in range(2):
                        b = pstart(("smp", 3 * hp + z))
                        pe.wait_ge(S("s_terms"), 2 * hp + z + 1)
                        pdone(("smp", 3 * hp + z), pe.matmul(b[:, :], bdones, (sq1, sq2)[z].rearrange("p a b -> p (a b)"),
                                                             start=True, stop=True))
                else:
                    hp = step[1]
                    b = pstart(("smp", 3 * hp + 2))
                    pe.wait_ge(S("s_read"), hp + 1)
                    pdone(("smp", 3 * hp + 2), pe.matmul(b[:, :], bdones, sq3.rearrange("p a b -> p (a b)"),
                                                         start=True, stop=True))
            pe.wait_ge(S("e_Y"), NCH)
            pe.wait_ge(S("s_fold"), NB)
            heads_sum("gnm", yy)
            pe.wait_ge(S("gn_square"), 1)
            heads_sum("gnv", scr2)
            w = arrived(("g2", 0))
            for n in range(NB):
                b = pstart(("g2", n))
                pdone(("g2", n), pe.matmul(b[:, 0:T], w[:, n * 128:(n + 1) * 128], tg, start=True, stop=True))
            pe.wait_ge(S("gn_out"), 1)
            dense("wo", lambda m: ("wo", m), lambda k: oo[:, k, :])
            pe.wait_ge(S("square"), 2)
            channel_sum(scr)

            def hidden(nm, keyf, count, taken, full):
                for n in range(count):
                    b, b2 = pstart((nm, n)), bank[4 + n % 2]
                    wait(pe, taken, n - 1)
                    w = arrived(keyf(n)).rearrange("p (o k c) -> p o k c", o=2, k=NB)
                    for k in range(NB):
                        ins = pe.matmul(b[:, 0:T], w[:, 0, k, :], h[:, k, 1:T + 1], start=(k == 0), stop=(k == NB - 1))
                    pdone((nm, n), ins)
                    for k in range(NB):
                        ins = pe.matmul(b2[:, 0:T], w[:, 1, k, :], h[:, k, 1:T + 1], start=(k == 0), stop=(k == NB - 1))
                    ins.then_inc(S(full), 1)

            pe.wait_ge(S("hadd"), 2 * NB)
            pe.wait_ge(S("hsamp"), 2)
            hidden("up", lambda n: ("up", n), NF, "ff_h", "ff_up")
            for n in range(NB):
                b = pstart(("down", n))
                for hh in range(2):
                    w = arrived(("down", 2 * n + hh)).rearrange("p (k c) -> p k c", k=FE)
                    for k in range(FE):
                        if n == 0:
                            pe.wait_ge(S("ff_h"), FE * hh + k + 1)
                        ins = pe.matmul(b[:, 0:T], w[:, k, :], ff[:, FE * hh + k, :], start=(hh == 0 and k == 0),
                                        stop=(hh == 1 and k == FE - 1))
                pdone(("down", n), ins)
            pe.wait_ge(S("square"), 3)
            channel_sum(scr)

            pe.wait_ge(S("hadd"), 3 * NB)
            pe.wait_ge(S("hsamp"), 3)
            hidden("pw1", lambda n: ("pw1", n), NB, "glu_gate", "glu_mm")
            for m in range(NB - NV):
                pwait_taken(pe, ("pw1", NV + m))
                for w in range(CW):
                    q = CW * m + w
                    if w == 0 or q in DIAGS:
                        pe.wait_ge(S("diag"), sum(d <= q for d in DIAGS))
                    ins = pe.matmul(bank[2 + m][:, 0:SEQ], diag[:, q % NDG, :], upad[:, NV + m, w:w + SEQ],
                                    start=(w == 0), stop=(w == CW - 1))
                ins.then_inc(S("conv_mm"), 1)
            pe.wait_ge(S("conv_ev"), NB - NV)
            pe.wait_ge(S("conv_done"), 1)
            channel_sum(zz)
            pe.wait_ge(S("ln_square"), 1)
            channel_sum(scr)
            pe.wait_ge(S("z_ready"), NB)
            dense("pw2", lambda m: ("pw2", m), lambda k: zz[:, k, :])
            pe.wait_ge(S("square"), 4)
            channel_sum(scr)

            pe.wait_ge(S("hadd"), 4 * NB)
            pe.wait_ge(S("hsamp"), 4)
            pe.wait_ge(S("router_in"), 32)
            pwait_taken(pe, ("pw2", NB - 1))
            pwait_taken(pe, ("pw2", NB - 2))
            for t, (a, b_) in enumerate(TOK):
                o = bank[0][0:b_ - a, 16 * t:16 * t + NE]
                for k in range(NB):
                    pe.matmul(o, h[:, k, 1 + a:1 + b_], rwt[:, k, :], start=(k == 0), stop=False)
                ins = pe.matmul(o, ones[0:1, 0:b_ - a], rbr[0:1, :], start=False, stop=True)
            ins.then_inc(S("logits"), 1)
            for t, (a, b_) in enumerate(TOK):
                for g in range(2):
                    q = 2 * t + g
                    wait(pe, "tok_ev", q - 1)
                    for j in range(4):
                        ins = pe.transpose(bank[2 + q % 2][0:b_ - a, 128 * j:128 * j + 128],
                                           h[:, 4 * g + j, 1 + a:1 + b_], ident)
                    ins.then_inc(S("tokmajor"), 1)
            pe.wait_ge(S("ranks_in"), 1)
            for t, (a, b_) in enumerate(TOK):
                o = bank[0][0:b_ - a, 64 + 16 * t:64 + 16 * t + NE]
                for t2 in range(t):
                    pe.matmul(o, ones[:, 0:b_ - a], msk[:, t2, :], start=(t2 == 0), stop=False)
                pe.matmul(o, tri[0:b_ - a, 0:b_ - a], msk[0:b_ - a, t, :], start=(t == 0), stop=True)
            for t, (a, b_) in enumerate(TOK):
                ins = pe.matmul(bank[0][:, 128:128 + NE], ones[0:b_ - a, :], msk[0:b_ - a, t, :], start=(t == 0),
                                stop=(t == 2))
            ins.then_inc(S("ranked"), 1)
            pe.wait_ge(S("tok_ev"), 6)

            def gather(j):
                pe.wait_ge(S("sel"), j + 1)
                for g in range(2):
                    for q in range(4):
                        for t, (a, b_) in enumerate(TOK):
                            ins = pe.matmul(bank[4 + g][:, CAP * q:CAP * q + CAP],
                                            htm[0:b_ - a, t, 128 * (4 * g + q):128 * (4 * g + q) + 128],
                                            sel[0:b_ - a, t, :], start=(t == 0), stop=(t == 2))
                    ins.then_inc(S("gath"), 1)

            def down(j, f):
                pe.wait_ge(S("hev"), j * FE + f + 1)
                if f == 0:
                    wait(pe, "y_ev", j * 2)
                for o in range(2):
                    ins = pe.matmul(bank[2 + o][0:CAP, :], he[:, f, :],
                                    ring3[f][:, 2 * D + 512 * o:2 * D + 512 * o + 512], start=(f == 0),
                                    stop=(f == FE - 1))
                ins.then_inc(S("job"), 1)

            def job(j):
                pe.wait_ge(S("xe_ev"), (j + 1) * 2)
                for f in range(FE):
                    pe.wait_ge(mslot_in[f], (j + 1) * 16)
                    w = ring3[f].rearrange("p (o k c) -> p o k c", o=3, k=NB)
                    if f >= 2:
                        pe.wait_ge(S("hev"), j * FE + f - 1)
                    for o in range(2):
                        for k in range(NB):
                            ins = pe.matmul(bank[f % 2][:, CAP * o:CAP * o + CAP], w[:, o, k, :], h[:, k, 0:CAP],
                                            start=(k == 0), stop=(k == NB - 1))
                    ins.then_inc(S("w13"), 1)
                    if f >= 1:
                        down(j, f - 1)
                down(j, FE - 1)
                gather(j + 1)
                pe.wait_ge(S("selg"), j + 1)
                wait(pe, "scat_ev", j * NB)
                for t, (a, b_) in enumerate(TOK):
                    ins = pe.transpose(bank[7][0:CAP, a:b_], selg[0:b_ - a, t, :], ident[0:b_ - a, 0:b_ - a])
                ins.then_inc(S("sel_t"), 1)
                pe.wait_ge(S("y_ev"), (j + 1) * 2)
                pe.wait_ge(S("selt_ev"), j + 1)
                for n in range(NB):
                    if n >= 2:
                        pe.wait_ge(S("scat_ev"), j * NB + n - 1)
                    pe.matmul(bank[6 + n % 2][:, 0:T], yout[0:CAP, 128 * n:128 * n + 128], selt[0:CAP, :],
                              start=True, stop=True).then_inc(S("scat"), 1)

            gather(0)
            job(0)
            with pe.Fori(1, NE) as j:
                job(j)
            pe.wait_ge(S("joblist"), 1)
            extra = pe.value_load(jobi[0:1, 0:1], min_val=0, max_val=NJ - NE)
            with pe.If(extra > 0):
                with pe.Fori(NE, extra + NE) as j:
                    job(j)
            pe.wait_ge(S("square"), 5)
            channel_sum(scr)

        @block.scalar
        def _(act):
            A = act.activation

            def taken(key, ins):
                ins.then_inc(pfree[pbank(key)[1]], 1)

            def pcopy(key, out, func=ACT.Copy, rows=128, cols=T, **kw):
                pwait_full(act, key)
                b = pbank(key)[0]
                taken(key, A(out, b[0:rows, 0:cols], func, **kw))

            def ada(n):
                if n >= 28:
                    return
                act.wait_ge(S("ada_mm"), 2 * n + 2)
                wait(act, "ada_tr", n - 1)
                A(arow[0:NC, n % 2, :], bank[6][0:NC, :], ACT.Copy).then_inc(S("ada_row"), 1)

            def norm(i, sums, shift, dst):
                if i == 1:
                    act.wait_ge(S("x_in"), 16)
                else:
                    act.wait_ge(S("x_new"), i - 1)
                A(scr[:, :, :], x[:, :, :], ACT.Square).then_inc(S("square"), 1)
                act.wait_ge(S("norm_sum"), sums)
                A(rtmp, bank[7][:, 128:128 + T], ACT.Sqrt, bias=eps[:, 0:1], scale=1.0 / D).then_inc(S("norm_root"), 1)
                for k in range(NB):
                    act.wait_ge(S("hmul"), (i - 1) * NB + k + 1)
                    A(dst(k)[:, 0:SEQ], dst(k)[:, 0:SEQ], ACT.Identity, bias=mod[:, shift + k, 0:1])\
                        .then_inc(S("hadd"), 1)

            act.wait_ge(S("c_in"), 16)
            A(csil[:, :, :], csil[:, :, :], ACT.Silu).then_inc(S("csil"), 1)
            act.wait_ge(S("consts"), 1)
            for n in range(12):
                ada(n)
            hk = lambda k: h[:, k, 1:T + 1]
            norm(1, 1, 0, hk)
            act.wait_ge(S("shb_ready"), 1)
            act.dma_start(io["shift_out"], shb[:, :, :]).then_inc(S("shift_o"), 16)
            pcopy(("lw1", 0), ex[0:64, 0, :], ACT.Tanh, rows=64)
            pwait_full(act, ("la1", 0))
            taken(("la1", 0), A(ex[64:128, 0, :], pbank(("la1", 0))[0][64:128, 0:T], ACT.Copy))
            pcopy(("lg1", 0), tg, ACT.Sigmoid)
            for n in range(NB):
                pcopy(("w", n), lw[:, n, :], ACT.Sigmoid, bias=pc("w0", n))
            for n in range(NB):
                pcopy(("a", n), att[:, n, :], ACT.Sigmoid, bias=pc("a0", n))
            for n in range(NB):
                pcopy(("k", n), ktt[:, n, :])
            for n in range(NB):
                pcopy(("kks", n), tmp[:, n, :], ACT.Sqrt)
            for n in range(NB):
                pcopy(("r", n), rt[:, n, :])
            for n in range(NB):
                pcopy(("bon", n), scr[:, n, :])
            for n in range(NB):
                pcopy(("v", n), vt[:, n, :])
            act.wait_ge(S("p1_ready"), 1)
            A(ex[:, :, :], cum[:, :, :], ACT.Exp).then_inc(S("expc"), 1)
            A(lw[:, :, :], lw[:, :, :], ACT.Exp).then_inc(S("expc"), 1)
            A(cum[:, :, :], cum[:, :, :], ACT.Exp, scale=-1.0).then_inc(S("expc"), 1)

            COPY = {"P2": sabd, "P2T": vbd, "P4": p_, "P4T": pt_, "P8": sabd, "Btm": btm, "Ktm": ktm, "Vtm": vbd,
                    "W": ww_, "W2": ww_}
            for step in STEPS:
                if step[0] == "ada":
                    ada(step[1])
                elif step[0] == "sample_a":
                    for z in range(2):
                        key = ("smp", 3 * step[1] + z)
                        pcopy(key, (sq1, sq2)[z].rearrange("p a b -> p (a b)"), cols=512)
                elif step[0] == "prod":
                    _, c, nm = step
                    if nm in COPY:
                        for g in range(2):
                            b, i, u = gbank(c, nm, g)
                            act.wait_ge(cfull[i], u)
                            A(COPY[nm][:, 4 * g:4 * g + 4, :], b.rearrange("p (a b) -> p a b", a=4), ACT.Copy)\
                                .then_inc(S("e_" + nm), 1)
                        if nm == "Vtm":
                            act.wait_ge(S("e_Vtm"), 2 * c + 2)
                            for q in range(2):
                                ins = A(vst[64 * q:64 * q + 64, :, :], vbd[64 * q:64 * q + 64, :, 64 * q:64 * q + 64],
                                        ACT.Copy)
                            ins.then_inc(S("e_Vst"), 1)
                    elif nm in ("X", "SA", "Y"):
                        b, i, u = gbank(c, nm, 0)
                        act.wait_ge(cfull[i], u)
                        dst = {"X": xst, "SA": sast, "Y": yy[:, :, C * c:C * c + C]}[nm]
                        A(dst[:, :, :], b.rearrange("p (a b) -> p a b", a=8), ACT.Copy).then_inc(S("e_" + nm), 1)
            act.wait_ge(S("e_S0"), NCH + 1)
            act.dma_start(io["wkv_out"], s0st[:, :, :]).then_inc(S("wkv_o"), 16)
            for n in range(NB):
                pcopy(("gnm", n), gmean[:, n, :], scale=1.0 / C)
            act.wait_ge(S("gn_centered"), 1)
            A(scr2[:, :, :], yy[:, :, :], ACT.Square).then_inc(S("gn_square"), 1)
            for n in range(NB):
                pcopy(("gnv", n), gmean[:, n, :], ACT.Sqrt, bias=eps[:, 1:2], scale=1.0 / C)
            for n in range(NB):
                pcopy(("g2", n), gg[:, n, :])
            norm(2, 2, 24, hk)
            for n in range(NF):
                wait(act, "ff_h", n - 1)
                pcopy(("up", n), glf[:, n % 2, :], ACT.Silu)
            norm(3, 3, 48, hk)
            for n in range(NB):
                act.wait_ge(S("glu_mm"), n + 1)
                if n >= 2:
                    pwait_taken(act, ("pw1", n - 2))
                A(gl[:, n % 2, :], bank[4 + n % 2][:, 0:T], ACT.Sigmoid, bias=pc("pw1_b", NB + n))\
                    .then_inc(S("glu_gate"), 1)
            pwait_taken(act, ("pw1", NB - 1))
            act.dma_start(io["convp"], upad[:, :, SEQ:SEQ + CW - 1]).then_inc(S("conv_o"), 16)
            act.dma_start(io["convs"], cbuf[:, :, 1:CW]).then_inc(S("conv_o"), 16)
            for m in range(NB - NV):
                act.wait_ge(S("conv_mm"), m + 1)
                A(zz[:, NV + m, 0:SEQ], bank[2 + m][:, 0:SEQ], ACT.Identity, bias=pc("dw_b", NV + m))\
                    .then_inc(S("conv_ev"), 1)
            act.wait_ge(S("norm_sum"), 4)
            A(rtmp, bank[7][:, 128:128 + T], ACT.Copy, scale=1.0 / D).then_inc(S("ln_mean"), 1)
            act.wait_ge(S("ln_centered"), 1)
            A(scr[:, :, :], zz[:, :, :], ACT.Square).then_inc(S("ln_square"), 1)
            act.wait_ge(S("norm_sum"), 5)
            A(rtmp, bank[7][:, 128:128 + T], ACT.Sqrt, bias=eps[:, 2:3], scale=1.0 / D).then_inc(S("ln_root"), 1)
            act.wait_ge(S("ln_scaled"), 1)
            for n in range(NB):
                A(zz[:, n, :], zz[:, n, :], ACT.Silu, bias=pc("ln_b", n), scale=pc("ln_g", n))\
                    .then_inc(S("z_ready"), 1)
            norm(4, 6, 72, hk)
            act.wait_ge(S("conv_o"), 32)
            for t, (a, b_) in enumerate(TOK):
                for g in range(2):
                    act.wait_ge(S("tokmajor"), 2 * t + g + 1)
                    A(htm[0:b_ - a, t, 512 * g:512 * g + 512], bank[2 + g][0:b_ - a, :], ACT.Copy)\
                        .then_inc(S("tok_ev"), 1)
            act.wait_ge(S("diff"), 1)
            A(sc2[:, :, 0:1], sc1[:, :, 0:1], ACT.Exp).then_inc(S("ediff"), 1)

            def gathered(j):
                for g in range(2):
                    act.wait_ge(S("gath"), j * 2 + g + 1)
                    A(h[:, 4 * g:4 * g + 4, 0:CAP], bank[4 + g][:, 0:4 * CAP].rearrange("p (a b) -> p a b", a=4),
                      ACT.Copy).then_inc(S("xe_ev"), 1)

            def job(j):
                for f in range(FE):
                    act.wait_ge(S("w13"), j * FE + f + 1)
                    if f >= 2:
                        act.wait_ge(S("hev"), j * FE + f - 1)
                    else:
                        wait(act, "hev", j * FE + f - 1)
                    A(silm[:, f % 2, :], bank[f % 2][:, 0:CAP], ACT.Silu).then_inc(S("sil"), 1)
                act.wait_ge(S("job"), (j + 1) * FE)
                wait(act, "scat", j * NB)
                for o in range(2):
                    A(yout[0:CAP, 512 * o:512 * o + 512], bank[2 + o][0:CAP, :], ACT.Copy).then_inc(S("y_ev"), 1)
                gathered(j + 1)
                act.wait_ge(S("sel_t"), j + 1)
                A(selt[0:CAP, :], bank[7][0:CAP, 0:T], ACT.Copy).then_inc(S("selt_ev"), 1)

            gathered(0)
            job(0)
            with act.Fori(1, NE) as j:
                job(j)
            act.wait_ge(S("joblist"), 1)
            extra = act.value_load(jobi[0:1, 0:1], min_val=0, max_val=NJ - NE)
            with act.If(extra > 0):
                with act.Fori(NE, extra + NE) as j:
                    job(j)
            norm(5, 7, 96, lambda k: scr[:, k, :])

        @block.vector
        def _(dve):
            chain = [0]

            def link(ins):
                chain[0] += 1
                ins.then_inc(S("dve_chain"), 1)
                dve.wait_ge(S("dve_chain"), chain[0])

            TT, TS, STT = dve.tensor_tensor, dve.tensor_scalar, dve.scalar_tensor_tensor

            def bc(v, n):
                return v.unsqueeze(2).to_broadcast([v.shape[0], v.shape[1], n])

            def mid(v, n):
                return v.unsqueeze(1).to_broadcast([v.shape[0], n, v.shape[1]])

            def ada(n):
                if n:
                    m = n - 1
                    dve.wait_ge(S("ada_tr"), m + 1)
                    o = (m % 2) * 4 * NC
                    TT(mod[:, 4 * m:4 * m + 4, :], bank[7][:, o:o + 4 * NC].rearrange("p (a b) -> p a b", a=4),
                       bc(adab[:, 4 * m:4 * m + 4], NC), ALU.add).then_inc(S("ada_ev"), 1)

            adab = par[:, PCOL["ada_b"]:PCOL["ada_b"] + 112]

            def norm(i, shift, scale, g, dst, wide):
                dve.wait_ge(S("ada_ev"), 12 if i < 3 else 24 if i < 5 else 28)
                link(STT(gain[:, :, :], mod[:, scale:scale + NB, :], 1.0, bc(g, NC), ALU.add, ALU.mult))
                dve.wait_ge(S("norm_root"), i)
                link(dve.reciprocal(rstd, rtmp))
                link(TT(smt[:, 0, :, :], x[:, :, SEQ:T], mid(rstd[:, SEQ:T], NB), ALU.mult))
                link(TT(smt[:, 1, :, :], smt[:, 0, :, :], gain[:, :, 1:NC], ALU.mult))
                TT(wide, smt[:, 1, :, :], mod[:, shift:shift + NB, 1:NC], ALU.add).then_inc(S("hsamp"), 1)
                for k in range(NB):
                    STT(dst(k)[:, 0:SEQ], x[:, k, 0:SEQ], gain[:, k, 0:1], rstd[:, 0:SEQ], ALU.mult, ALU.mult)\
                        .then_inc(S("hmul"), 1)

            def residual(b, n, gate, done, bias=None):
                g0, gs = mod[:, gate + n, 0:1], mod[:, gate + n, 1:NC]
                if bias is None:
                    STT(x[:, n, 0:SEQ], b[:, 0:SEQ], g0, x[:, n, 0:SEQ], ALU.mult, ALU.add)
                    link(TT(smt[:, 0, n, :], b[:, SEQ:T], gs, ALU.mult))
                else:
                    TS(scr[:, n, 0:SEQ], b[:, 0:SEQ], bias, g0, ALU.add, ALU.mult)
                    link(STT(smt[:, 0, n, :], b[:, SEQ:T], bias, gs, ALU.add, ALU.mult))
                    TT(x[:, n, 0:SEQ], scr[:, n, 0:SEQ], x[:, n, 0:SEQ], ALU.add)
                done(TT(x[:, n, SEQ:T], smt[:, 0, n, :], x[:, n, SEQ:T], ALU.add))

            def taken(key):
                return lambda ins: ins.then_inc(pfree[pbank(key)[1]], 1)

            dve.wait_ge(S("consts"), 1)
            dve.memset(eps[:, 0:1], RMS_EPS)
            dve.memset(eps[:, 1:2], GN_EPS)
            dve.memset(eps[:, 2:3], LN_EPS)
            dve.memset(h[:, :, 0:1], 0.0)
            dve.wait_ge(S("par_in"), 16)
            for n in range(13):
                ada(n)
            norm(1, 0, 8, pc("norm_mix_g", 0, NB), lambda k: h[:, k, 1:T + 1], h[:, :, SEQ + 1:T + 1])
            dve.wait_ge(S("hadd"), NB)
            dve.wait_ge(S("shift_in"), 16)
            TT(xx[:, :, 0:SEQ], h[:, :, 0:SEQ], h[:, :, 1:SEQ + 1], ALU.subtract)
            TT(xx[:, :, SEQ:T], shf[:, :, :], h[:, :, SEQ + 1:T + 1], ALU.subtract).then_inc(S("xx"), 1)
            dve.wait_ge(S("xx"), 1)
            dve.tensor_copy(shb[:, :, :], h[:, :, SEQ:T + 1]).then_inc(S("shb_ready"), 1)

            def mixture(q, m, after):
                if after:
                    pwait_full(dve, after)
                for k in range(NB):
                    ins = STT(xi[q % 2][:, k, :], xx[:, k, :], pc("mu", m * NB + k), h[:, k, 1:T + 1],
                              ALU.mult, ALU.add)
                ins.then_inc(S("xi"), 1)

            mixture(0, 1, None)
            mixture(1, 4, None)
            mixture(2, 5, ("lw1", 0))
            mixture(3, 2, ("la1", 0))
            mixture(4, 0, ("lg1", 0))
            pwait_taken(dve, ("w", NB - 1))
            link(TS(lw[:, :, :], lw[:, :, :], DECAY, None, ALU.mult))
            for n in range(NB):
                dve.tensor_tensor_scan(cum[:, n, :], scanm, lw[:, n, :], 0.0, ALU.mult, ALU.add)
            pwait_taken(dve, ("k", NB - 1))
            pwait_taken(dve, ("k", NB - 2))
            link(TT(btt[:, :, :], ktt[:, :, :], bc(pc("kk", 0, NB), T), ALU.mult))
            TT(scr[:, :, :], btt[:, :, :], btt[:, :, :], ALU.mult).then_inc(S("kk_sq"), 1)
            mixture(5, 3, ("k", NB - 1))
            link(TS(ex[:, :, :], att[:, :, :], -1.0, None, ALU.add))
            link(TT(ex[:, :, :], ex[:, :, :], bc(pc("ka", 0, NB), T), ALU.mult))
            link(STT(ktt[:, :, :], ex[:, :, :], 1.0, ktt[:, :, :], ALU.add, ALU.mult))
            pwait_taken(dve, ("kks", NB - 1))
            pwait_taken(dve, ("kks", NB - 2))
            link(TS(tmp[:, :, :], tmp[:, :, :], 1e-12, None, ALU.max))
            link(dve.reciprocal(tmp[:, :, :], tmp[:, :, :]))
            link(STT(btt[:, :, :], btt[:, :, :], -1.0, tmp[:, :, :], ALU.mult, ALU.mult))
            link(STT(att[:, :, :], btt[:, :, :], -1.0, att[:, :, :], ALU.mult, ALU.mult))
            pwait_taken(dve, ("r", NB - 1))
            pwait_taken(dve, ("r", NB - 2))
            link(TT(tmp[:, :, :], rt[:, :, :], ktt[:, :, :], ALU.mult))
            TT(tmp[:, :, :], tmp[:, :, :], bc(pc("rk", 0, NB), T), ALU.mult).then_inc(S("rk_prod"), 1)
            for k, v in enumerate((rt, None, ktt, None, btt, att)):
                if v is not None:
                    dve.tensor_copy(smp[:, k * NB:(k + 1) * NB, :], v[:, :, SEQ:T])
            TT(lw[:, :, :], cum[:, :, :], lw[:, :, :], ALU.subtract).then_inc(S("p1_ready"), 1)
            pwait_taken(dve, ("v", NB - 1))
            pwait_taken(dve, ("v", NB - 2))
            dve.tensor_copy(smp[:, 3 * NB:4 * NB, :], vt[:, :, SEQ:T])
            TT(bonus[:, :, :], scr[:, :, :], vt[:, :, :], ALU.mult)
            dve.wait_ge(S("expc"), 1)
            dve.tensor_copy(smp[:, NB:2 * NB, :], ex[:, :, SEQ:T]).then_inc(S("zeros"), 1)
            TT(rt[:, :, :], rt[:, :, :], ex[:, :, :], ALU.mult)
            for c in range(NCH):
                dve.tensor_copy(ecl[:, :, c:c + 1], ex[:, :, C * c + C - 1:C * c + C])
            dve.wait_ge(S("expc"), 2)
            TT(btt[:, :, :], btt[:, :, :], lw[:, :, :], ALU.mult)
            dve.wait_ge(S("expc"), 3)
            TT(att[:, :, :], att[:, :, :], cum[:, :, :], ALU.mult)
            link(TT(ktt[:, :, :], ktt[:, :, :], cum[:, :, :], ALU.mult))
            pwait_full(dve, ("v", NB - 1))
            for v in (abd, bbd, kbd, ww_, sabd, s0bd, s0st):
                ins = dve.memset(v[:, :, :], 0.0)
            ins.then_inc(S("e_S0"), 1)
            dve.wait_ge(S("e_S0"), 1)

            def half(dst, src, col=None):
                for q in range(2):
                    p = slice(64 * q, 64 * q + 64)
                    s = src[p, :, :] if col is None else src[p, :, col:col + C]
                    ins = dve.tensor_copy(dst[p, :, 64 * q:64 * q + 64], s)
                return ins

            MASK = {"M": [(p_, m_p, "P")], "MT": [(pt_, m_pt, "PT"), (m32, m_32t, "M32"), (m64, m_64t, "M64")],
                    "NT": [(ntm, m_su, "NT")]}
            ADD = {"T2": tt_, "T3": tt_, "T4": tt_, "T5": tt_, "U2": uu_, "U3": uu_, "U4": uu_, "U5": uu_, "U6": uu_}
            for step in STEPS:
                if step[0] == "start":
                    c = step[1]
                    if c:
                        b, i, u = gbank(c - 1, "S", 0)
                        dve.wait_ge(cfull[i], u)
                    half(abd, btt, C * c)
                    half(bbd, att, C * c).then_inc(S("chunk_d"), 1)
                elif step[0] == "ada" and step[1] > 12:
                    ada(step[1])
                elif step[0] == "sample_b":
                    hp = step[1]
                    key = ("smp", 3 * hp + 2)
                    pwait_full(dve, key)
                    v = TT(sq3[:, :, :], pbank(key)[0].rearrange("p (a b) -> p a b", a=NS), mid(id64, NS), ALU.mult)
                    taken(key)(v)
                    pwait_taken(dve, key)
                    dve.tensor_reduce(yy[:, hp, SEQ:T], sq3[:, :, :], AX, ALU.add).then_inc(S("s_fold"), 1)
                elif step[0] == "prod":
                    _, c, nm = step
                    if nm in MASK:
                        for g in range(2):
                            b, i, u = gbank(c, nm, g)
                            dve.wait_ge(cfull[i], u)
                            hs = slice(4 * g, 4 * g + 4)
                            for dst, m, name in MASK[nm]:
                                TT(dst[:, hs, :], b.rearrange("p (a b) -> p a b", a=4), mid(m, 4), ALU.mult)\
                                    .then_inc(S("e_" + name), 1)
                        if nm == "M":
                            dve.wait_ge(S("e_P"), 2 * c + 2)
                            TT(tt_[:, :, :], p_[:, :, :], mid(ident, NB), ALU.add).then_inc(S("e_T1"), 1)
                        if nm == "MT":
                            dve.wait_ge(S("e_PT"), 2 * c + 2)
                            for g in range(2):
                                TT(uu_[:, 4 * g:4 * g + 4, :], pt_[:, 4 * g:4 * g + 4, :], mid(ident, 4), ALU.add)\
                                    .then_inc(S("e_U1"), 1)
                    elif nm in ("QBT", "QKT"):
                        b, i, u = gbank(c, nm, 0)
                        dve.wait_ge(cfull[i], u)
                        TT((qbt if nm == "QBT" else qkt)[:, :, :], b.rearrange("p (a b) -> p a b", a=8), mid(m_iu, 8),
                           ALU.mult).then_inc(S("e_" + nm), 1)
                    elif nm in ADD:
                        if nm == "T2":
                            dve.wait_ge(S("e_T1"), c + 1)
                        elif nm == "U2":
                            dve.wait_ge(S("e_U1"), 2 * c + 2)
                        else:
                            dve.wait_ge(S("e_" + nm[0] + str(int(nm[1]) - 1)), 2 * c + 2)
                        for g in range(2):
                            b, i, u = gbank(c, nm, g)
                            dve.wait_ge(cfull[i], u)
                            hs = slice(4 * g, 4 * g + 4)
                            TT(ADD[nm][:, hs, :], b.rearrange("p (a b) -> p a b", a=4), ADD[nm][:, hs, :], ALU.add)\
                                .then_inc(S("e_" + nm), 1)
                    elif nm == "SA":
                        dve.wait_ge(S("e_SA"), c + 1)
                        half(sabd, sast).then_inc(S("e_SAbd"), 1)
                    elif nm == "S":
                        b, i, u = gbank(c, nm, 0)
                        dve.wait_ge(cfull[i], u)
                        link(TT(s0st[:, :, :], b.rearrange("p (a b) -> p a b", a=8), s0st[:, :, :], ALU.add))
                        link(TT(s0st[:, :, :], s0st[:, :, :], ecl[:, :, c:c + 1].to_broadcast([128, NB, C]), ALU.mult))
                        half(s0bd, s0st).then_inc(S("e_S0"), 1)
            dve.wait_ge(S("e_Y"), NCH)
            dve.wait_ge(S("s_fold"), NB)
            pwait_taken(dve, ("gnm", NB - 1))
            pwait_taken(dve, ("gnm", NB - 2))
            TT(yy, yy, gmean[:, :, :], ALU.subtract).then_inc(S("gn_centered"), 1)
            pwait_taken(dve, ("gnv", NB - 1))
            pwait_taken(dve, ("gnv", NB - 2))
            link(dve.reciprocal(gmean[:, :, :], gmean[:, :, :]))
            link(TT(yy, yy, gmean[:, :, :], ALU.mult))
            for n in range(NB):
                ins = TS(oo[:, n, :], yy[:, n, :], pc("lnx_g", n), pc("lnx_b", n), ALU.mult, ALU.add)
            link(ins)
            link(TT(oo[:, :, :], oo[:, :, :], bonus[:, :, :], ALU.add))
            pwait_taken(dve, ("g2", NB - 1))
            pwait_taken(dve, ("g2", NB - 2))
            TT(oo[:, :, :], oo[:, :, :], gg[:, :, :], ALU.mult).then_inc(S("gn_out"), 1)
            for n in range(NB):
                pwait_full(dve, ("wo", n))
                residual(pbank(("wo", n))[0], n, 16, taken(("wo", n)))

            def x_done():
                dve.tensor_copy(eps[:, 3:4], x[:, NB - 1, T - 1:T]).then_inc(S("x_new"), 1)

            pwait_taken(dve, ("wo", NB - 1))
            x_done()
            norm(2, 24, 32, pc("norm_ffn_g", 0, NB), lambda k: h[:, k, 1:T + 1], h[:, :, SEQ + 1:T + 1])
            for n in range(NF):
                pwait_taken(dve, ("up", n))
                dve.wait_ge(S("ff_up"), n + 1)
                TT(ff[:, n, :], bank[4 + n % 2][:, 0:T], glf[:, n % 2, :], ALU.mult).then_inc(S("ff_h"), 1)
            for n in range(NB):
                pwait_full(dve, ("down", n))
                residual(pbank(("down", n))[0], n, 40, taken(("down", n)))
            pwait_taken(dve, ("down", NB - 1))
            x_done()
            norm(3, 48, 56, pc("norm_mix_g", NB, NB), lambda k: h[:, k, 1:T + 1], h[:, :, SEQ + 1:T + 1])
            dve.wait_ge(S("s_out"), 16 * NB)
            dve.wait_ge(S("wkv_o"), 16)
            dve.memset(upad[:, :, 0:CW - 1], 0.0)
            dve.wait_ge(S("conv_in"), 16)
            dwp = par[:, PCOL["dw"]:PCOL["dw"] + NB * CW].rearrange("p (n w) -> p n w", n=NB)
            taps = [(n + q, w) for n in range(0, NV, 2) for w in range(CW) for q in range(2)]
            done = [0]

            def convolve(upto):
                for k in range(done[0], upto):
                    n, w = taps[k]
                    if w == 0:
                        pwait_taken(dve, ("pw1", n))
                        ins = TS(zz[:, n, 0:SEQ], upad[:, n, 0:SEQ], dwp[:, n, 0:1], pc("dw_b", n), ALU.mult, ALU.add)
                    else:
                        dve.wait_ge(S("tap"), k - 1)
                        ins = STT(zz[:, n, 0:SEQ], upad[:, n, w:w + SEQ], dwp[:, n, w:w + 1], zz[:, n, 0:SEQ],
                                  ALU.mult, ALU.add)
                    ins.then_inc(S("tap"), 1)
                done[0] = upto

            for n in range(NB):
                dve.wait_ge(S("glu_gate"), n + 1)
                pwait_full(dve, ("pw1", n))
                b = pbank(("pw1", n))[0]
                STT(upad[:, n, CW - 1:CW - 1 + SEQ], b[:, 0:SEQ], pc("pw1_b", n), gl[:, n % 2, 0:SEQ], ALU.add, ALU.mult)
                taken(("pw1", n))(STT(cbuf[:, n * NS:(n + 1) * NS, CW - 1], b[:, SEQ:T], pc("pw1_b", n),
                                      gl[:, n % 2, SEQ:T], ALU.add, ALU.mult))
                if n:
                    convolve(TAPS * n)
            pwait_taken(dve, ("pw1", NB - 1))
            link(TT(cprd.rearrange("p (n b) w -> p n b w", n=NB), cbuf.rearrange("p (n b) w -> p n b w", n=NB),
                    dwp.unsqueeze(2).to_broadcast([128, NB, NS, CW]), ALU.mult))
            link(dve.tensor_reduce(smt[:, 0, :, :].rearrange("p a b -> p (a b)"), cprd[:, :, :], AX, ALU.add))
            TT(zz[:, :, SEQ:T], smt[:, 0, :, :], bc(pc("dw_b", 0, NB), NS), ALU.add)
            convolve(len(taps))
            dve.wait_ge(S("tap"), len(taps))
            dve.memset(eps[:, 3:4], 0.0).then_inc(S("conv_done"), 1)
            dve.wait_ge(S("ln_mean"), 1)
            dve.wait_ge(S("conv_done"), 1)
            dve.wait_ge(S("conv_ev"), NB - NV)
            TT(zz[:, :, :], zz[:, :, :], mid(rtmp, NB), ALU.subtract).then_inc(S("ln_centered"), 1)
            dve.wait_ge(S("ln_root"), 1)
            link(dve.reciprocal(rstd, rtmp))
            TT(zz[:, :, :], zz[:, :, :], mid(rstd, NB), ALU.mult).then_inc(S("ln_scaled"), 1)
            for n in range(NB):
                pwait_full(dve, ("pw2", n))
                residual(pbank(("pw2", n))[0], n, 64, taken(("pw2", n)), bias=pc("pw2_b", n))
            pwait_taken(dve, ("pw2", NB - 1))
            x_done()
            norm(4, 72, 80, pc("norm_ffn_g", NB, NB), lambda k: h[:, k, 1:T + 1], h[:, :, SEQ + 1:T + 1])

            link(dve.memset(lg[:, :, :], 0.0))
            dve.wait_ge(S("logits"), 1)
            b0 = bank[0][:, 0:48].rearrange("p (t e) -> p t e", t=3)
            dve.tensor_copy(lg[:, 0:2, :], b0[:, 0:2, 0:NE])
            link(dve.tensor_copy(lg[0:NS, 2:3, :], b0[0:NS, 2:3, 0:NE]))

            def best(src, m, oh):
                link(dve.tensor_reduce(m, src[:, :, :], AX, ALU.max))
                link(TT(sc1[:, :, :], src[:, :, :], bc(m, NE), ALU.is_equal))
                link(TT(sc1[:, :, :], sc1[:, :, :], mid(iota_e, 3), ALU.mult))
                link(dve.tensor_reduce(cur[:, 0:3], sc1[:, :, :], AX, ALU.max))
                link(TT(oh[:, :, :], sc1[:, :, :], bc(cur[:, 0:3], NE), ALU.is_equal))

            best(lg, mx[:, 0:3], oh1)
            link(STT(sc2[:, :, :], oh1[:, :, :], -3e38, lg[:, :, :], ALU.mult, ALU.add))
            best(sc2, mx[:, 3:6], oh2)
            TT(msk[:, :, :], oh1[:, :, :], oh2[:, :, :], ALU.add).then_inc(S("ranks_in"), 1)
            TT(sc1[:, :, 0], mx[:, 3:6], mx[:, 0:3], ALU.subtract).then_inc(S("diff"), 1)
            dve.wait_ge(S("ediff"), 1)
            link(TS(mx[:, 0:3], sc2[:, :, 0], 1.0, None, ALU.add))
            link(dve.reciprocal(mx[:, 0:3], mx[:, 0:3]))
            link(TT(mx[:, 3:6], mx[:, 0:3], sc2[:, :, 0], ALU.mult))
            link(TT(oh1[:, :, :], oh1[:, :, :], bc(mx[:, 0:3], NE), ALU.mult))
            link(TT(oh2[:, :, :], oh2[:, :, :], bc(mx[:, 3:6], NE), ALU.mult))
            dve.memset(jg[:, :, :], 0.0)
            dve.memset(jr[:, :, :], -BIG)
            link(dve.memset(sc2[:, :, :], 0.0))
            link(TT(jg[:, :, 0:NE], oh1[:, :, :], oh2[:, :, :], ALU.add))
            dve.wait_ge(S("ranked"), 1)
            rk = bank[0][:, 64:112].rearrange("p (t e) -> p t e", t=3)
            dve.tensor_copy(sc2[:, 0:2, :], rk[:, 0:2, 0:NE])
            dve.tensor_copy(cnt, bank[0][:, 128:128 + NE])
            link(dve.tensor_copy(sc2[0:NS, 2:3, :], rk[0:NS, 2:3, 0:NE]))
            link(STT(sc1[:, :, :], sc2[:, :, :], BIG, msk[:, :, :], ALU.add, ALU.mult))
            link(TS(jr[:, :, 0:NE], sc1[:, :, :], -BIG, None, ALU.add))

            def pick(j):
                dve.tensor_copy(cur[:, 0:3].unsqueeze(2), jr[:, :, bass.ds(j, 1)]).then_inc(S("curr"), 1)
                dve.wait_ge(S("curr"), j + 1)
                for t in range(3):
                    ins = TS(sel[:, t, :], iota_c, cur[:, t:t + 1], None, ALU.is_equal)
                ins.then_inc(S("sel"), 1)

            pick(0)
            for k in range(2):
                TS(rx[:, :, NE * k:NE * k + NE], sc1[:, :, :], -float(CAP * (k + 1)), None, ALU.add)
                dve.tensor_copy(gx[:, :, NE * k:NE * k + NE], jg[:, :, 0:NE])
                ins = TS(flg[:, NE * k:NE * k + NE], cnt, float(CAP * (k + 1)), None, ALU.is_gt)
            link(ins)
            link(dve.tensor_tensor_scan(pos, ones[:, 0:16], flg, 0.0, ALU.mult, ALU.add))
            for m in range(NJ - NE):
                link(STT(jm, pos, float(m + 1), flg, ALU.is_equal, ALU.mult))
                link(TT(jt[:, :, :], rx[:, :, :], mid(jm, 3), ALU.mult))
                link(dve.tensor_reduce(cur[:, 3:6], jt[:, :, :], AX, ALU.add))
                TS(jr[:, :, NE + m], cur[:, 3:6], -BIG, None, ALU.add)
                link(TT(jt[:, :, :], gx[:, :, :], mid(jm, 3), ALU.mult))
                dve.tensor_reduce(jg[:, :, NE + m], jt[:, :, :], AX, ALU.add)
                link(TT(jm, jm, eidx, ALU.mult))
                link(dve.tensor_reduce(jobf[:, m + 1:m + 2], jm, AX, ALU.add))
            link(dve.tensor_copy(jobf[:, 0:1], pos[:, 15:16]))
            dve.tensor_copy(jobi[0:1, 0:NJ - NE + 1], jobf[0:1, 0:NJ - NE + 1]).then_inc(S("joblist"), 1)
            dve.wait_ge(S("joblist"), 1)

            def job(j):
                dve.tensor_copy(cur[:, 3:6].unsqueeze(2), jg[:, :, bass.ds(j, 1)]).then_inc(S("curg"), 1)
                dve.wait_ge(S("curg"), j + 1)
                wait(dve, "sel_t", j)
                for t in range(3):
                    ins = TS(selg[:, t, :], iota_c, cur[:, t:t + 1], cur[:, 3 + t:4 + t], ALU.is_equal, ALU.mult)
                ins.then_inc(S("selg"), 1)
                dve.wait_ge(S("gath"), 2 * j + 2)
                dve.wait_ge(S("selg"), j + 1)
                pick(j + 1)
                for f in range(FE):
                    dve.wait_ge(S("sil"), j * FE + f + 1)
                    TT(he[:, f, :], bank[f % 2][:, CAP:2 * CAP], silm[:, f % 2, :], ALU.mult).then_inc(S("hev"), 1)
                for n in range(NB):
                    dve.wait_ge(S("scat"), j * NB + n + 1)
                    b = bank[6 + n % 2]
                    STT(x[:, n, 0:SEQ], b[:, 0:SEQ], mod[:, 88 + n, 0:1], x[:, n, 0:SEQ], ALU.mult, ALU.add)
                    TT(smt[:, 0, n, :], b[:, SEQ:T], mod[:, 88 + n, 1:NC], ALU.mult).then_inc(S("scat_ev"), 1)
                dve.wait_ge(S("scat_ev"), j * NB + NB)
                TT(x[:, :, SEQ:T], smt[:, 0, :, :], x[:, :, SEQ:T], ALU.add).then_inc(S("x_job"), 1)
                dve.wait_ge(S("x_job"), j + 1)

            job(0)
            with dve.Fori(1, NE) as j:
                job(j)
            extra = dve.value_load(jobi[0:1, 0:1], min_val=0, max_val=NJ - NE)
            with dve.If(extra > 0):
                with dve.Fori(NE, extra + NE) as j:
                    job(j)
            x_done()
            norm(5, 96, 104, pc("final_g", 0, NB), lambda k: scr[:, k, :], scr[:, :, SEQ:T])

        @block.gpsimd
        def _(pool):
            chain = [0]

            def link(ins):
                chain[0] += 1
                ins.then_inc(S("pool_chain"), 1)
                pool.wait_ge(S("pool_chain"), chain[0])

            AS = pool.affine_select

            def where(out, src, base_, step, cm, op=ALU.is_ge, fill=0.0):
                pat = [[step, out.shape[1]]] if isinstance(step, int) else step
                link(AS(out=out, in_=src, compare_op=op, fill=fill, base=base_, pattern=pat, channel_multiplier=cm))

            pool.memset(ones, 1.0)
            pool.memset(bdones, 0.0)
            pool.memset(m_iu, 1.0)
            pool.memset(scanm, 1.0)
            link(pool.memset(ident, 0.0))
            for q in range(2):
                link(pool.memset(bdones[64 * q:64 * q + 64, 64 * q:64 * q + 64], 1.0))
            for c in range(NCH):
                pool.memset(scanm[:, C * c:C * c + 1], 0.0)
            link(pool.memset(scanm[:, SEQ:T], 0.0))
            where(ident, ident, 0, -1, 1, ALU.not_equal, 1.0)
            where(tri, ones, -1, 1, -1)
            for q in range(2):
                p = slice(64 * q, 64 * q + 64)
                where(m_iu[p, :], m_iu[p, :], 0, 1, -1)
                link(pool.tensor_copy(id64[p, :], ident[p, 64 * q:64 * q + 64]))
            for m, w in ((m_pt, 16), (m_32t, 32)):
                v = m.rearrange("p (a b) -> p a b", b=w)
                o = ones.rearrange("p (a b) -> p a b", b=w)
                link(AS(out=v, in_=o, compare_op=ALU.is_ge, fill=0.0, base=0, pattern=[[-w, 128 // w], [0, w]],
                        channel_multiplier=1))
                link(AS(out=v, in_=v, compare_op=ALU.is_ge, fill=0.0, base=w - 1, pattern=[[w, 128 // w], [0, w]],
                        channel_multiplier=-1))
            where(m_p, m_pt, -1, -1, 1)
            where(m_pt, m_pt, -1, 1, -1)
            where(m_32t, m_32t, -1, 1, -1)
            where(m_su, bdones, -1, 1, -1)
            link(pool.tensor_tensor(m_64t, m_su, m_32t, ALU.subtract))
            link(pool.tensor_tensor(m_32t, m_32t, m_pt, ALU.subtract))
            pool.iota(iota_c, pattern=[[1, CAP]], base=0, channel_multiplier=0, allow_small_or_imprecise_dtypes=True)
            pool.iota(iota_e, pattern=[[-1, NE]], base=NE, channel_multiplier=0, allow_small_or_imprecise_dtypes=True)
            link(pool.iota(eidx, pattern=[[0, 2], [1, NE]], base=0, channel_multiplier=0,
                           allow_small_or_imprecise_dtypes=True))
            pool.memset(arow[:, 0, 0:1], 0.0).then_inc(S("consts"), 1)

            pool.wait_ge(S("zeros"), 1)
            TTp = pool.tensor_tensor

            def vec(k, hp):
                return smp[:, k * NB + hp, :].unsqueeze(2).to_broadcast([128, NS, C])

            def load(hp):
                if hp >= 2:
                    pool.wait_ge(S("s_out"), 16 * (hp - 1))
                pool.dma_start(sst[hp % 2][:, :, :], io["state"][hp]).then_inc(S("s_in"), 16)

            def terms(hp):
                s = sst[hp % 2]
                pool.wait_ge(S("s_in"), 16 * (hp + 1))
                if hp:
                    pwait_full(pool, ("smp", 3 * hp - 1))
                TTp(sq1[:, :, :], s[:, :, :], vec(4, hp), ALU.mult).then_inc(S("s_terms"), 1)
                TTp(sq2[:, :, :], id64.unsqueeze(1).to_broadcast([128, NS, C]), vec(3, hp), ALU.mult)\
                    .then_inc(S("s_terms"), 1)

            load(0)
            for step in STEPS:
                if step[0] == "start":
                    c = step[1]
                    if c:
                        b, i, u = gbank(c - 1, "S", 0)
                        pool.wait_ge(cfull[i], u)
                        pool.wait_ge(S("s_terms"), 4 * c + 2)
                    else:
                        pool.wait_ge(S("e_S0"), 1)
                    for q in range(2):
                        p = slice(64 * q, 64 * q + 64)
                        if q:
                            link(ins)
                        for dst, src in ((kbd, ktt), (ww_, vt)):
                            ins = pool.tensor_copy(dst[p, :, 64 * q:64 * q + 64], src[p, :, C * c:C * c + C])
                    ins.then_inc(S("chunk_p"), 1)
                    pool.wait_ge(S("chunk_p"), c + 1)
                    if c == 0:
                        terms(0)
                elif step[0] == "sample_a":
                    hp = step[1]
                    s = sst[hp % 2]
                    if hp + 1 < NB:
                        load(hp + 1)
                    pwait_taken(pool, ("smp", 3 * hp))
                    pwait_taken(pool, ("smp", 3 * hp + 1))
                    TTp(sq1[:, :, :], sq1[:, :, :], vec(5, hp), ALU.mult)
                    TTp(sq2[:, :, :], sq2[:, :, :], vec(2, hp), ALU.mult)
                    link(TTp(s[:, :, :], s[:, :, :], vec(1, hp), ALU.mult))
                    link(TTp(s[:, :, :], s[:, :, :], sq1[:, :, :], ALU.add))
                    link(TTp(s[:, :, :], s[:, :, :], sq2[:, :, :], ALU.add))
                    if hp:
                        pool.wait_ge(S("s_fold"), hp)
                    TTp(sq3[:, :, :], s[:, :, :], vec(0, hp), ALU.mult).then_inc(S("s_read"), 1)
                    pool.dma_start(io["state_out"][hp], s[:, :, :]).then_inc(S("s_out"), 16)
                    if hp + 1 < NB:
                        terms(hp + 1)
            pwait_full(pool, ("down", NB - 1))
            pdw = par[:, PCOL["dw"]:PCOL["dw"] + NB * CW]
            for q, end in zip(DIAGS, DIAGS[1:] + [CW * (NB - NV)]):
                for a, e in ((q, min(end, q - q % NDG + NDG)), (q - q % NDG + NDG, end)):
                    if a < e:
                        if a >= NDG:
                            pool.wait_ge(S("conv_mm"), (e - 1 - NDG) // CW + 1)
                        n = e - a
                        ins = TTp(diag[:, a % NDG:a % NDG + n, :], ident.unsqueeze(1).to_broadcast([128, n, 128]),
                                  pdw[:, NV * CW + a:NV * CW + e].unsqueeze(2).to_broadcast([128, n, 128]), ALU.mult)
                ins.then_inc(S("diag"), 1)


def _blocks(w):
    k, n = w.shape
    return w.reshape(k // 128, 128, n // 128, 128).transpose(2, 1, 0, 3)


def _rows(v):
    return v.reshape(-1, 128).T


def _cols(w):
    n = w.shape[1] // 512
    return w.reshape(2, 4, 128, n, 512).transpose(3, 0, 2, 1, 4).reshape(2 * n, 128, 4 * 512)


def _layout(np, a):
    f = {k: np.asarray(v) for k, v in a.items()}
    arr = {}
    arr["ada"] = np.concatenate([_cols(f["ada_w"][0]), _cols(f["ada_w"][1]), _cols(f["final_ada_w"])])
    pair = lambda w: _blocks(w).reshape(-1, 2, 128, w.shape[0]).transpose(0, 2, 1, 3).reshape(-1, 128, 2 * w.shape[0])
    arr["rkv"] = np.concatenate([pair(f["rw_wk"][0]), pair(f["rw_wr"][0]), pair(f["rw_wv"][0])])
    arr["wo"] = pair(f["rw_wo"][0])
    arr["pw2"] = pair(f["cv_pw2_w"][0])
    arr["g2"] = f["rw_g2"][0]
    both = lambda u, v: np.concatenate([_blocks(u).reshape(-1, 128, u.shape[0]), _blocks(v).reshape(-1, 128, v.shape[0])], 2)
    arr["up"] = both(f["ffn_w1"][0], f["ffn_w3"][0])
    arr["pw1"] = both(f["cv_pw1_w"][0][:, :D], f["cv_pw1_w"][0][:, D:])
    w2 = _blocks(f["ffn_w2"][0])
    arr["down"] = w2.reshape(NB, 128, 2, FE * 128).transpose(0, 2, 1, 3).reshape(2 * NB, 128, FE * 128)
    arr["moe"] = np.concatenate([
        np.concatenate([both(f["moe_w1"][0, e], f["moe_w3"][0, e]), f["moe_w2"][0, e].reshape(FE, 128, D)], 2)
        for e in range(NE)])
    lo = np.concatenate([f["rw_w1"][0], f["rw_a1"][0], f["rw_g1"][0]], 1)
    arr["lo1"] = lo.reshape(NB, 128, 256).transpose(1, 0, 2)
    arr["lo2"] = np.concatenate([f["rw_w2"][0], f["rw_a2"][0]])
    arr["rw"] = f["moe_router_w"][0].reshape(NB, 128, NE).transpose(1, 0, 2)
    arr["rb"] = f["moe_router_b"]
    dw = f["cv_dw_w"][0].reshape(CW, NB, 128).transpose(2, 1, 0).reshape(128, NB * CW)
    arr["par"] = np.concatenate([_rows(f[k]) for k in (
        "ada_b", "final_ada_b", "norm_mix_g", "norm_ffn_g", "rw_mu", "rw_w0", "rw_a0", "rw_kk", "rw_ka", "rw_rk",
        "rw_lnx_g", "rw_lnx_b", "cv_pw1_b", "cv_dw_b", "cv_ln_g", "cv_ln_b", "cv_pw2_b", "final_g")] + [dw], 1)
    feat = lambda v: v.reshape(-1, NB, 128).transpose(2, 1, 0)
    arr["x"] = feat(np.concatenate([f["x_prompt"][0], f["x_sample"][:, 0]]))
    arr["c"] = feat(np.concatenate([f["c_prompt"], f["c_sample"]]))
    arr["shift"] = feat(f["state_shift"][0])
    arr["conv"] = f["state_conv"][0].reshape(NS, CW - 1, NB, 128).transpose(3, 2, 0, 1).reshape(128, NB * NS, CW - 1)
    arr["state"] = f["state_wkv"][0].reshape(NS, NB, 2, C, C).transpose(1, 2, 4, 0, 3).reshape(NB, 128, NS, C)
    return {k: np.ascontiguousarray(v) for k, v in arr.items()}


_OUTS = {"y": (128, NB, T), "shift_out": (128, NB, NC), "wkv_out": (128, NB, C), "state_out": (NB, 128, NS, C),
         "convp": (128, NB, CW - 1), "convs": (128, NB * NS, CW - 1)}


def kernel(**inputs):
    import numpy as np
    import concourse.bacc as bacc
    from concourse.bass_utils import run_bass_kernel_spmd

    arrays = _layout(np, inputs)
    nc = bacc.Bacc("TRN2", target_bir_lowering=False, num_devices=1)
    io = {k: nc.dram_tensor("in_" + k, a.shape, mybir.dt.from_np(a.dtype), kind="ExternalInput").ap()
          for k, a in arrays.items()}
    io.update({k: nc.dram_tensor("out_" + k, s, F32, kind="ExternalOutput").ap() for k, s in _OUTS.items()})
    build(nc, io)
    got = run_bass_kernel_spmd(nc, [{"in_" + k: a for k, a in arrays.items()}], core_ids=[0]).results[0]
    r = {k: got["out_" + k] for k in _OUTS}
    y = r["y"].transpose(2, 1, 0).reshape(T, D)
    sh = r["shift_out"].transpose(2, 1, 0).reshape(NC, D)
    wkv = r["wkv_out"].reshape(2, C, NB, C).transpose(2, 0, 3, 1).reshape(1, 1, 2 * NB, C, C)
    wkv_s = r["state_out"].reshape(NB, 2, C, NS, C).transpose(3, 0, 1, 4, 2).reshape(1, NS, 2 * NB, C, C)
    cp = r["convp"].transpose(2, 1, 0).reshape(1, 1, CW - 1, D)
    cs = r["convs"].reshape(128, NB, NS, CW - 1).transpose(2, 3, 1, 0).reshape(1, NS, CW - 1, D)
    out = (y[None, :SEQ], y[SEQ:, None], wkv, sh[None, :1], cp, wkv_s, sh[None, 1:], cs)
    return tuple(np.ascontiguousarray(v) for v in out)
```

```python
from contextlib import ExitStack

import concourse.bass as bass
from concourse import mybir

F32 = mybir.dt.float32
I32 = mybir.dt.int32
ALU = mybir.AluOpType
ACT = mybir.ActivationFunctionType
AX = mybir.AxisListType.X

D = 1024
NB = D // 128
SEQ = 256
NS = 8
T = SEQ + NS
NC = 1 + NS
C = 64
NCH = SEQ // C
CW = 31
TAPS = 18
NG = 1
NV = 6
NF = 22
NE = 8
FE = 11
CAP = 96
NJ = NE + (2 * T) // CAP
BIG = 4096.0
RMS_EPS, LN_EPS, GN_EPS = 1e-6, 1e-5, 64e-5
DECAY = -0.6065306597126334

PCOL, _n = {}, 0
for _name, _w in (("ada_b", 112), ("norm_mix_g", 16), ("norm_ffn_g", 16), ("mu", 48), ("w0", 8), ("a0", 8),
                  ("kk", 8), ("ka", 8), ("rk", 8), ("lnx_g", 8), ("lnx_b", 8), ("pw1_b", 16), ("dw_b", 8),
                  ("ln_g", 8), ("ln_b", 8), ("pw2_b", 8), ("final_g", 8), ("dw", NB * CW)):
    PCOL[_name] = _n
    _n += _w
NPAR = _n

SLOT = 2048
MSLOT = 3 * D


def plan_stream():
    plan = []
    for n, key in enumerate([("ada", n) for n in range(12)] + [("rkv", n) for n in range(12)]
                            + [("ada", n) for n in range(12, 56)] + [("g2", 0)] + [("wo", n) for n in range(4)]):
        plan.append((key, D if key[0] == "g2" else SLOT, n % 4))
    first = len(plan)
    order = list(range(4, 12)) + list(range(4))
    then = [("up", n) for n in range(NF)] + [("down", n) for n in range(2 * NB)]
    for n, key in enumerate(then):
        plan.append((key, FE * 128 if key[0] == "down" else SLOT, order[n % 12]))
    late = [s for s in (order[(len(then) + n) % 12] for n in range(12)) if s < 8]
    plan += [(("pw1", n), SLOT, late[n]) for n in range(8)]
    plan += [(("pw2", n), SLOT, 8 + n) for n in range(4)]
    return plan, first


def build(nc, io):
    ctx = ExitStack()
    with ctx:
        arena = ctx.enter_context(nc.sbuf_tensor("arena", [128, 53100], F32))
        top = [0]

        def at(off, *shape):
            n = 1
            for s in shape:
                n *= s
            v = arena[:, off:off + n]
            if len(shape) == 2:
                v = v.rearrange("p (a b) -> p a b", a=shape[0])
            if len(shape) == 3:
                v = v.rearrange("p (a b c) -> p a b c", a=shape[0], b=shape[1])
            return v

        def keep(*shape):
            n = 1
            for s in shape:
                n *= s
            v = at(top[0], *shape)
            top[0] += n
            return v

        x = keep(NB, T)
        h = keep(NB, T + 1)
        par = keep(NPAR)
        mod = keep(112, NC)
        ident = keep(128)
        ones = keep(128)
        bdones = keep(128)
        m_su = keep(128)
        m_iu = keep(C)
        m_p = keep(128)
        m_pt = keep(128)
        m_32t = keep(128)
        m_64t = keep(128)
        scanm = keep(T)
        scr = keep(NB, T)
        rstd = keep(T)
        rtmp = keep(T)
        gain = keep(NB, NC)
        smt = keep(2, NB, NS)
        eps = keep(4)
        csil = keep(NB, NC)
        tg = keep(T)
        arow = keep(2, 512)
        id64 = keep(C)
        tri = keep(128)
        iota_c = keep(CAP)
        iota_e = keep(NE)
        eidx = keep(16)
        shb = keep(NB, NC)
        shf = keep(NB, NS)
        rwt = keep(NB, NE)
        rbr = keep(NE)
        tset = keep(2)
        base = top[0]

        ring1 = [at(base + SLOT * n, SLOT) for n in range(4)]
        rw = base + 4 * SLOT
        rt, vt, att, btt, ktt = (at(rw + 2112 * n, NB, T) for n in range(5))
        ck = rw + 5 * 2112
        assert ck + 2112 * 3 >= base + 12 * SLOT
        xx = at(ck, NB, T)
        xi = [at(ck + 2112 * (1 + n), NB, T) for n in range(2)]
        lw = at(ck + 2112 * 3, NB, T)
        cum = at(ck + 2112 * 4, NB, T)
        ex = at(ck + 2112 * 5, NB, T)
        tmp = at(ck + 2112 * 6, NB, T)
        lo1 = at(ck + 2112 * 7, NB, 256)
        lo2 = at(ck + 2112 * 7 + 2048, D)
        st = [at(ck + C * NB * n, NB, C) for n in range(26)]
        p_, pt_, m32, m64, pp_, ppt, p4_, p4t, tt_, ww_, xst, sast = st[:12]
        uu, nt, qbt, qkt, btm, ktm, vtm = (st[12 + 2 * n:14 + 2 * n] for n in range(7))
        s0st = at(ck + 1024 * 18, NB, C)
        sp0 = ck + 1024 * 19
        smp = at(sp0, 6 * NB, NS)
        sst = [at(sp0 + 384 + 512 * n, NS, C) for n in range(2)]
        sq1, sq2, sq3 = (at(sp0 + 384 + 1024 + 512 * n, NS, C) for n in range(3))
        ecl = at(sp0 + 384 + 2560, NB, NCH)
        assert sp0 + 384 + 2560 + 32 <= 53100
        yy = h[:, :, 1:T + 1]
        bonus = scr
        oo, scr2 = (at(ck + 2112 * n, NB, T) for n in (4, 5))
        gg = at(ck + C * NB * 26, NB, T)
        hsum = at(ck + C * NB * 26 + 2112, NB, 16)
        hrep = at(ck + C * NB * 26 + 2240, NB, 128)
        gsd = at(ck + C * NB * 26 + 3264, T)
        assert C * NB * 26 + 3264 + T <= 1024 * 18
        ring2 = [at(base + SLOT * n, SLOT) for n in range(12)]
        r2e = base + 12 * SLOT
        ff = at(r2e, NF, T)
        cvb = r2e + NF * T
        upad = at(cvb, NB, SEQ + CW - 1)
        zz = at(cvb + NB * (SEQ + CW - 1), NB, T)
        cbuf = at(cvb + NB * (SEQ + CW - 1) + 2112, NB * NS, CW)
        cprd = at(cvb + NB * (SEQ + CW - 1) + 2112 + NB * NS * CW, NB * NS, CW)
        gtap = at(cvb + NB * (SEQ + CW - 1) + 2112 + 2 * NB * NS * CW, 2, SEQ)
        glf = at(cvb, 2, T)
        gl = at(r2e, 2, T)
        NDG = (NF * T - 2 * T) // 128
        diag = at(r2e + 2 * T, NDG, 128)
        ring3 = [at(base + MSLOT * n, MSLOT) for n in range(FE)]
        mo = base + FE * MSLOT
        htm = at(mo, 3, D)
        he = at(mo + 3072, FE, CAP)
        sel = at(mo + 3072 + 1056, 3, CAP)
        selg = at(mo + 3072 + 1056 + 288, 3, CAP)
        selt = at(mo + 3072 + 1056 + 576, T)
        yout = at(mo + 3072 + 1056 + 576 + 264, D)
        mt0 = mo + 3072 + 1056 + 576 + 264 + 1024
        lg = at(mt0, 3, NE)
        sc1 = at(mt0 + 24, 3, NE)
        sc2 = at(mt0 + 48, 3, NE)
        oh1 = at(mt0 + 72, 3, NE)
        oh2 = at(mt0 + 96, 3, NE)
        msk = at(mt0 + 120, 3, NE)
        jr = at(mt0 + 144, 3, NJ + 1)
        jg = at(mt0 + 144 + 42, 3, NJ + 1)
        cur = at(mt0 + 228, 6)
        cnt = at(mt0 + 340, NE)
        flg = at(mt0 + 348, 16)
        pos = at(mt0 + 364, 16)
        jm = at(mt0 + 380, 16)
        rx = at(mt0 + 412, 3, 16)
        gx = at(mt0 + 460, 3, 16)
        jt = at(mt0 + 508, 3, 16)
        jobf = at(mt0 + 556, 8)
        mx = at(mt0 + 564, 6)
        silm = at(mt0 + 644, 2, CAP)
        assert mt0 + 644 + 192 <= 53100, mt0 + 964
        jobi = ctx.enter_context(nc.sbuf_tensor("jobi", [1, 8], I32))

        bank = [ctx.enter_context(nc.psum_tensor(f"bank{n}", [128, 512], F32)) for n in range(8)]
        SEMS = """consts masks c_in csil par_in x_in lora_in shift_in conv_in router_in ada_mm ada_row ada_tr ada_ev
            square norm_sum norm_root hmul hadd hsamp hscaled xx xi kk_sq rk_prod p1_ready expc zeros e_P e_PT
            e_M32 e_M64 e_U1 e_NT e_QBT e_QKT e_U2 e_U3 e_T4 e_U4 e_T5 e_U5 e_U6 e_P2 e_P2T e_P4 e_P4T e_P8
            e_Btm e_Ktm e_Vtm e_W e_W2 e_X e_SA e_Y e_S0 s_in s_out s_terms s_read s_fold heads_ready
            gn_square gn_sum gn_root gn_rstd gn_mid gn_out ff_up ff_h x_new glu_gate glu_mm conv_done tap
            tap_g tapped_g diag conv_mm conv_ev ln_mean ln_centered ln_square ln_root ln_scaled z_ready logits
            tokmajor tok_ev ranks_in ranked sel selg gath xe_ev w13 sil hev job y_ev sel_t selt_ev scat
            scat_ev curr curg x_job diff ediff joblist y_out shift_o wkv_o conv_o shb_ready table dve_chain
            pool_chain""".split()
        sems = {name: ctx.enter_context(nc.semaphore(name)) for name in SEMS}
        S = sems.__getitem__
        slot_in = [ctx.enter_context(nc.semaphore(f"slot_in{n}")) for n in range(12)]
        mslot_in = [ctx.enter_context(nc.semaphore(f"mslot_in{n}")) for n in range(FE)]
        cfull = [ctx.enter_context(nc.semaphore(f"chunk_bank_full{n}")) for n in range(4)]
        pfull = [ctx.enter_context(nc.semaphore(f"out_bank_full{n}")) for n in range(2)]
        pfree = [ctx.enter_context(nc.semaphore(f"out_bank_free{n}")) for n in range(2)]

        def wait(eng, name, val):
            if not (isinstance(val, int) and val <= 0):
                eng.wait_ge(sems[name], val)

        plan, n_first = plan_stream()
        piece_of, occupant, used = {}, {}, [0] * 12
        before = []
        for key, w, s in plan:
            used[s] += 1
            before.append(occupant.get(s))
            occupant[s] = key
            ring = ring1 if len(before) <= n_first else ring2
            piece_of[key] = (ring[s][:, 0:w], s, 16 * used[s])

        def pc(name, b, n=1):
            o = PCOL[name] + b
            return par[:, o:o + n]

        HEAD = """M MT X- q NT q P2 P2T q SA- q QBT U2 q P4 P4T q Y- q S- q QKT q U3
            q P8 sample_a q Btm U4 q Ktm q Vtm q T4 q W q sample_b U5 sample_a q T5 q W2 q U6 sample_b q""".split()
        STEPS, quarter, n_sa, n_sb = [], 4 * 6, 0, 0

        def ada_quarter():
            nonlocal quarter
            STEPS.append(("ada" if quarter % 4 == 3 else "quarter", quarter // 4, quarter % 4))
            quarter += 1

        for c in range(NCH):
            for nm in HEAD:
                if nm == "q":
                    ada_quarter()
                elif nm == "sample_a":
                    STEPS.append((nm, n_sa))
                    n_sa += 1
                elif nm == "sample_b":
                    STEPS.append((nm, n_sb))
                    n_sb += 1
                elif nm[-1] != "-":
                    STEPS.append(("prod", c, nm))
                elif c:
                    STEPS.append(("prod", c - 1, nm[:-1]))
        for nm in "q q X q q SA q q g2 Y S q q".split():
            if nm == "q":
                ada_quarter()
            else:
                STEPS.append((nm,) if nm == "g2" else ("prod", NCH - 1, nm))
        STEPS.append(("ada", 28, 3))
        GORD = [st_[1:] for st_ in STEPS if st_[0] == "prod"]
        GK = {key: k for k, key in enumerate(GORD)}
        LAST = {"M": "P", "MT": "M64", "S": "S0"}

        def gbank(c, nm):
            k = GK[c, nm]
            return bank[2 + k % 4], k % 4, k // 4 + 1

        def gfree(c, nm):
            k = GK[c, nm] - 4
            if k < 0:
                return None
            c, nm = GORD[k]
            return "e_" + LAST.get(nm, nm), c + 1 + (nm == "S")

        PORD = []
        for nm, k in (("lw1", 1), ("la1", 1), ("lg1", 1), ("w", NB), ("a", NB), ("k", NB), ("r", 4), ("kks", NB), ("r", NB),
                      ("v", 4), ("bon", NB), ("v", NB), ("smp", 3 * NB), ("g2", NB), ("gnm", NB), ("gnb", NB), ("wo", NB),
                      ("up", NF), ("down", NB), ("pw1", NB), ("pw2", NB)):
            PORD += [(nm, n) for n in range(k) if (nm, n) not in PORD]
        PK = {key: k for k, key in enumerate(PORD)}

        def pbank(key):
            k = PK[key]
            return bank[k % 2], k % 2, k // 2 + 1

        def pwait_full(eng, key):
            eng.wait_ge(pfull[pbank(key)[1]], pbank(key)[2])

        def pwait_taken(eng, key):
            eng.wait_ge(pfree[pbank(key)[1]], pbank(key)[2])

        def consumed(eng, key):
            kind, n = key
            if kind == "ada":
                eng.wait_ge(S("ada_mm"), n + 1)
            elif kind == "rkv":
                pwait_full(eng, ("krv"[n // 4], 2 * (n % 4) + 1))
            elif kind in ("wo", "pw2"):
                pwait_full(eng, (kind, 2 * n + 1))
            elif kind == "g2":
                pwait_full(eng, ("g2", NB - 1))
            elif kind == "up":
                eng.wait_ge(S("ff_up"), n + 1)
            elif kind == "pw1":
                eng.wait_ge(S("glu_mm"), n + 1)
            elif kind == "down":
                pwait_full(eng, ("down", n // 2))

        DIAGS = sorted({CW * m for m in range(NB - NV)} | {q for q in range(NDG, CW * (NB - NV), NDG)})

        TAPS_V = []
        for n in range(NG, NV, 2):
            TAPS_V += [(n + q, w) for w in range(CW) for q in range(min(2, NV - n))]
        TAP_AT = {t: k for k, t in enumerate(TAPS_V)}
        SCAT = (6, 2, 3, 7)
        TOK = [(0, 128), (128, 256), (256, T)]
        block = ctx.enter_context(nc.Block())

        @block.sync
        def _(sp):
            sp.dma_start(csil[:, :, :], io["c"]).then_inc(S("c_in"), 16)
            for n, (key, w, s) in enumerate(plan):
                if before[n]:
                    consumed(sp, before[n])
                if n == n_first:
                    sp.wait_ge(cfull[gbank(NCH - 1, "S")[1]], gbank(NCH - 1, "S")[2])
                dst, _, _ = piece_of[key]
                src = io[key[0]] if key[0] == "g2" else io[key[0]][key[1]]
                sp.dma_start(dst, src).then_inc(slot_in[s], 16)
                if n == 1:
                    sp.dma_start(par, io["par"]).then_inc(S("par_in"), 16)
                if n == 3:
                    sp.dma_start(x[:, :, :], io["x"]).then_inc(S("x_in"), 16)
                if n == 7:
                    sp.dma_start(shf[:, :, :], io["shift"]).then_inc(S("shift_in"), 16)
                    sp.dma_start(lo1[:, :, :], io["lo1"]).then_inc(S("lora_in"), 16)
                    sp.dma_start(lo2, io["lo2"]).then_inc(S("lora_in"), 16)
                if key == ("up", 8):
                    pwait_taken(sp, ("wo", NB - 1))
                    sp.dma_start(cbuf[:, :, 0:CW - 1], io["conv"]).then_inc(S("conv_in"), 16)
                    sp.dma_start(rwt[:, :, :], io["rw"]).then_inc(S("router_in"), 16)
                    sp.dma_start(rbr[0:1, :], io["rb"]).then_inc(S("router_in"), 16)
            last = {s: key for key, w, s in plan}
            for f in range(FE):
                for s in range(12):
                    if s * SLOT < (f + 1) * MSLOT and f * MSLOT < (s + 1) * SLOT:
                        consumed(sp, last[s])
                if (f + 1) * MSLOT > 12 * SLOT:
                    pwait_full(sp, ("pw2", NB - 1))
                    sp.wait_ge(S("conv_o"), 32)
                sp.dma_start(ring3[f], io["moe"][f]).then_inc(mslot_in[f], 16)

            def stream(expert, j):
                for f in range(FE):
                    sp.wait_ge(S("job"), (j - 1) * FE + f + 1)
                    sp.dma_start(ring3[f], io["moe"][bass.ds(expert * FE + f, 1), :, :]
                                 .rearrange("a p n -> (a p) n")).then_inc(mslot_in[f], 16)

            with sp.Fori(1, NE) as j:
                stream(j, j)
            sp.wait_ge(S("joblist"), 1)
            extra = sp.value_load(jobi[0:1, 0:1], min_val=0, max_val=NJ - NE)
            with sp.If(extra > 0):
                with sp.Fori(0, extra) as m:
                    expert = sp.value_load(jobi[0:1, bass.ds(m + 1, 1)], min_val=0, max_val=NE - 1)
                    stream(expert, m + NE)
            for n in range(NB):
                sp.wait_ge(S("hadd"), 4 * NB + n + 1)
                sp.wait_ge(S("hsamp"), 5)
                sp.dma_start(io["y"][:, n, :], scr[:, n, :]).then_inc(S("y_out"), 16)
            sp.wait_ge(S("y_out"), 16 * NB)
            sp.wait_ge(S("shift_o"), 16)
            sp.wait_ge(S("wkv_o"), 16)
            sp.wait_ge(S("s_out"), 16 * NB)
            sp.wait_ge(S("conv_o"), 32)

        @block.tensor
        def _(pe):
            def arrived(key):
                dst, s, v = piece_of[key]
                pe.wait_ge(slot_in[s], v)
                return dst

            def pstart(key):
                b, i, u = pbank(key)
                if u > 1:
                    pe.wait_ge(pfree[i], u - 1)
                return b

            def pdone(key, ins):
                ins.then_inc(pfull[pbank(key)[1]], 1)

            def ada(n, parts=range(4)):
                if n < 28:
                    wait(pe, "ada_row", n)
                    for p in parts:
                        w = arrived(("ada", 2 * n + p // 2)).rearrange("p (k c) -> p k c", k=4)
                        for kb in range(2):
                            k = 2 * p + kb
                            ins = pe.matmul(bank[6][0:NC, :], csil[:, k, :], w[:, k % 4, :], start=(k == 0),
                                            stop=(k == NB - 1))
                        if p % 2:
                            ins.then_inc(S("ada_mm"), 1)
                if n and n != 4 and 3 in parts:
                    m = n - 1
                    pe.wait_ge(S("ada_row"), m + 1)
                    wait(pe, "ada_ev", m)
                    for j in range(4):
                        o = (m % 2) * 4 * NC + j * NC
                        ins = pe.transpose(bank[7][:, o:o + NC], arow[0:NC, m % 2, j * 128:(j + 1) * 128],
                                           ident[0:NC, 0:NC])
                    ins.then_inc(S("ada_tr"), 1)

            sums = [0]

            def channel_sum(src, ready, blocks=range(NB), b=bank[7]):
                for z, k in enumerate(blocks):
                    ready(k)
                    ins = pe.matmul(b[:, 128:128 + T], ones, src[:, k, :], start=(z == 0), stop=(z == NB - 1))
                ins.then_inc(S("norm_sum"), 1)

            def squares(i):
                return lambda k: pe.wait_ge(S("square"), NB * (i - 1) + k + 1)

            def modulated(i):
                def ready(k):
                    pe.wait_ge(S("hadd"), NB * (i - 1) + k + 1)
                    if k == 0:
                        pe.wait_ge(S("hsamp"), i)
                return ready

            def dense(nm, keyf, rhs, blocks=range(NB), ready=None):
                for n in blocks:
                    b = pstart((nm, n))
                    w = arrived(keyf(n // 2)).rearrange("p (o k c) -> p o k c", o=2, k=NB)
                    for k in range(NB):
                        if ready and n == 0:
                            ready(k)
                        ins = pe.matmul(b[:, 0:T], w[:, n % 2, k, :], rhs(k), start=(k == 0), stop=(k == NB - 1))
                    pdone((nm, n), ins)

            def heads_sum(nm, src):
                for n in range(NB):
                    b = pstart((nm, n))
                    pdone((nm, n), pe.matmul(b[:, 0:T], bdones, src[:, n, :], start=True, stop=True))

            pe.wait_ge(S("csil"), 1)
            ada(0)
            pe.wait_ge(S("consts"), 1)
            ada(1)
            ada(2)
            channel_sum(scr, squares(1), b=bank[5])
            ada(3)
            pe.wait_ge(S("ada_row"), 4)
            pe.wait_ge(S("ada_ev"), 3)
            for j in range(4):
                o = 4 * NC + j * NC
                ins = pe.transpose(bank[7][:, o:o + NC], arow[0:NC, 1, j * 128:(j + 1) * 128], ident[0:NC, 0:NC])
            ins.then_inc(S("ada_tr"), 1)
            ada(4)
            ada(5)

            pe.wait_ge(S("lora_in"), 32)
            for q, (nm, lo, hi) in enumerate((("lw1", 0, 64), ("la1", 64, 128), ("lg1", 128, 256))):
                b = pstart((nm, 0))
                pe.wait_ge(S("xi"), q + 1)
                o = b[64:128, 0:T] if nm == "la1" else b[0:hi - lo, 0:T]
                for k in range(NB):
                    ins = pe.matmul(o, lo1[:, k, lo:hi], xi[q % 2][:, k, :], start=(k == 0), stop=(k == NB - 1))
                pdone((nm, 0), ins)
            for q, nm in enumerate("wa"):
                pwait_taken(pe, (("lw1", 0), ("la1", 0))[q])
                for n in range(NB):
                    b = pstart((nm, n))
                    pdone((nm, n), pe.matmul(b[:, 0:T], lo2[64 * q:64 * q + 64, n * 128:(n + 1) * 128],
                                             ex[64 * q:64 * q + 64, 0, :], start=True, stop=True))
            pe.wait_ge(S("xi"), 4)
            dense("k", lambda m: ("rkv", m), lambda k: xi[1][:, k, :])
            pe.wait_ge(S("xi"), 5)
            dense("r", lambda m: ("rkv", 4 + m), lambda k: xi[0][:, k, :], range(4))
            pe.wait_ge(S("masks"), 1)
            pe.wait_ge(S("kk_sq"), 1)
            heads_sum("kks", scr)
            dense("r", lambda m: ("rkv", 4 + m), lambda k: xi[0][:, k, :], range(4, NB))
            pe.wait_ge(S("xi"), 6)
            dense("v", lambda m: ("rkv", 8 + m), lambda k: xi[1][:, k, :], range(4))
            pe.wait_ge(S("rk_prod"), 1)
            heads_sum("bon", tmp)
            dense("v", lambda m: ("rkv", 8 + m), lambda k: xi[1][:, k, :], range(4, NB))

            NEED = {
                "P2": ("PT", "P"), "P2T": ("PT", "P"), "U2": ("U1", "P2"), "P4": ("P2", "P2T"), "P4T": ("P2", "P2T"),
                "U3": ("U2", "P4"), "P8": ("P4", "P4T"), "U4": ("U3", "P8"), "T4": ("U4",), "W": ("M32", "T4"),
                "U5": ("U4", "W"), "T5": ("U5",), "W2": ("M64", "T5"), "U6": ("U5", "W2"), "X": ("NT", "S0", "Vtm"),
                "SA": ("U6", "X"), "Y": ("SA", "QBT", "QKT", "Vtm"), "S": ("Btm", "Ktm", "SA", "Vtm")}

            def tiles(c, nm):
                i = c % 2
                a, b, k, r = (v[:, :, C * c:C * c + C] for v in (btt, att, ktt, rt))
                return {
                    "M": [(a, b)], "MT": [(b, a)], "NT": [(k, a)], "QBT": [(b, r)], "QKT": [(k, r)],
                    "P2": [(pt_, p_)], "P2T": [(p_, pt_)], "U2": [(pp_, uu[i])], "P4": [(ppt, pp_)],
                    "P4T": [(pp_, ppt)], "U3": [(p4_, uu[i])], "P8": [(p4t, p4_)], "U4": [(pp_, uu[i])],
                    "W": [(m32, tt_)], "U5": [(ww_, uu[i])], "W2": [(m64, tt_)], "U6": [(ww_, uu[i])],
                    "X": [(a, s0st), (nt[i], vtm[i])], "SA": [(uu[i], xst)],
                    "Y": [(s0st, r), (sast, qbt[i]), (vtm[i], qkt[i])], "S": [(btm[i], sast), (ktm[i], vtm[i])]}[nm]

            def turned(c, nm):
                b, k, v = (v[:, :, C * c:C * c + C] for v in (att, ktt, vt))
                return {"Btm": b, "Ktm": k, "Vtm": v, "T4": uu[c % 2], "T5": uu[c % 2]}.get(nm)

            def prod(c, nm):
                b, i, u = gbank(c, nm)
                fr = gfree(c, nm)
                if fr:
                    pe.wait_ge(S(fr[0]), fr[1])
                if (c, nm) == (0, "Vtm"):
                    pwait_taken(pe, ("v", NB - 1))
                    pwait_taken(pe, ("v", NB - 2))
                if (c, nm) == (0, "M"):
                    pe.wait_ge(S("e_S0"), 1)
                for o_ in NEED.get(nm, ()):
                    pe.wait_ge(S("e_" + o_), c + 1)
                turn = turned(c, nm)
                pairs = [] if turn is not None else tiles(c, nm)
                for hp in range(NB):
                    for q in range(2):
                        p = slice(64 * q, 64 * q + 64)
                        o = b[p, C * hp:C * hp + C]
                        if turn is not None:
                            ins = pe.matmul(o, turn[p, hp, :], ident[p, p], start=True, stop=True)
                        for z, (l, r) in enumerate(pairs):
                            ins = pe.matmul(o, l[p, hp, :], r[p, hp, :], start=(z == 0), stop=(z == len(pairs) - 1))
                ins.then_inc(cfull[i], 1)

            for step in STEPS:
                if step[0] == "prod":
                    prod(step[1], step[2])
                elif step[0] == "g2":
                    w = arrived(("g2", 0))
                    for n in range(NB):
                        b = pstart(("g2", n))
                        pdone(("g2", n), pe.matmul(b[:, 0:T], w[:, n * 128:(n + 1) * 128], tg, start=True, stop=True))
                elif step[0] in ("quarter", "ada"):
                    ada(step[1], (step[2],))
                elif step[0] == "sample_a":
                    hp = step[1]
                    for z in range(2):
                        b = pstart(("smp", 3 * hp + z))
                        pe.wait_ge(S("s_terms"), 2 * hp + z + 1)
                        pdone(("smp", 3 * hp + z), pe.matmul(b[:, :], bdones, (sq1, sq2)[z].rearrange("p a b -> p (a b)"),
                                                             start=True, stop=True))
                else:
                    hp = step[1]
                    b = pstart(("smp", 3 * hp + 2))
                    pe.wait_ge(S("s_read"), hp + 1)
                    pdone(("smp", 3 * hp + 2), pe.matmul(b[:, :], bdones, sq3.rearrange("p a b -> p (a b)"),
                                                         start=True, stop=True))
            pe.wait_ge(S("e_Y"), NCH)
            pe.wait_ge(S("s_fold"), NB)
            heads_sum("gnm", yy)
            pe.wait_ge(S("heads_ready"), 1)
            for n in range(NB):
                pe.wait_ge(S("gn_square"), n + 1)
                ins = pe.matmul(bank[6][0:16, 0:T], hsum[:, n, :], scr2[:, n, :], start=(n == 0), stop=(n == NB - 1))
            ins.then_inc(S("gn_sum"), 1)
            pe.wait_ge(S("gn_rstd"), 1)
            for n in range(NB):
                b = pstart(("gnb", n))
                pdone(("gnb", n), pe.matmul(b[:, 0:T], hrep[0:16, n, :], gsd[0:16, :], start=True, stop=True))
            dense("wo", lambda m: ("wo", m), lambda k: oo[:, k, :], ready=lambda k: pe.wait_ge(S("gn_out"), k + 1))
            channel_sum(scr, squares(2))

            def hidden(nm, keyf, count, taken, full, ready):
                for n in range(count):
                    b, b2 = pstart((nm, n)), bank[4 + n % 2]
                    wait(pe, taken, n - 1)
                    w = arrived(keyf(n)).rearrange("p (o k c) -> p o k c", o=2, k=NB)
                    for k in range(NB):
                        if n == 0:
                            ready(k)
                        ins = pe.matmul(b[:, 0:T], w[:, 0, k, :], h[:, k, 1:T + 1], start=(k == 0), stop=(k == NB - 1))
                    pdone((nm, n), ins)
                    for k in range(NB):
                        ins = pe.matmul(b2[:, 0:T], w[:, 1, k, :], h[:, k, 1:T + 1], start=(k == 0), stop=(k == NB - 1))
                    ins.then_inc(S(full), 1)

            hidden("up", lambda n: ("up", n), NF, "ff_h", "ff_up", modulated(2))
            for n in range(NB):
                b = pstart(("down", n))
                for hh in range(2):
                    w = arrived(("down", 2 * n + hh)).rearrange("p (k c) -> p k c", k=FE)
                    for k in range(FE):
                        if n == 0:
                            pe.wait_ge(S("ff_h"), FE * hh + k + 1)
                        ins = pe.matmul(b[:, 0:T], w[:, k, :], ff[:, FE * hh + k, :], start=(hh == 0 and k == 0),
                                        stop=(hh == 1 and k == FE - 1))
                pdone(("down", n), ins)
            channel_sum(scr, squares(3))

            hidden("pw1", lambda n: ("pw1", n), NB, "glu_gate", "glu_mm", modulated(3))
            for m in range(NB - NV):
                pwait_taken(pe, ("pw1", NV + m))
                for w in range(CW):
                    q = CW * m + w
                    if w == 0 or q in DIAGS:
                        pe.wait_ge(S("diag"), sum(d <= q for d in DIAGS))
                    ins = pe.matmul(bank[2 + m][:, 0:SEQ], diag[:, q % NDG, :], upad[:, NV + m, w:w + SEQ],
                                    start=(w == 0), stop=(w == CW - 1))
                ins.then_inc(S("conv_mm"), 1)
            pe.wait_ge(S("conv_done"), 1)

            def convolved(k):
                if k < NG:
                    pe.wait_ge(S("tap_g"), (k + 1) * CW)
                elif k < NV:
                    pe.wait_ge(S("tap"), TAP_AT[k, CW - 1] + 1)
                else:
                    pe.wait_ge(S("conv_ev"), k - NV + 1)

            channel_sum(zz, convolved, list(range(NG, NV - 2)) + list(range(NV, NB)) + list(range(NG)) + [NV - 2, NV - 1])
            channel_sum(scr, lambda k: pe.wait_ge(S("ln_square"), k + 1))
            dense("pw2", lambda m: ("pw2", m), lambda k: zz[:, k, :], ready=lambda k: pe.wait_ge(S("z_ready"), k + 1))
            channel_sum(scr, squares(4))

            pe.wait_ge(S("router_in"), 32)
            ready = modulated(4)
            pwait_taken(pe, ("pw2", NB - 1))
            pwait_taken(pe, ("pw2", NB - 2))
            for t, (a, b_) in enumerate(TOK):
                o = bank[0][0:b_ - a, 16 * t:16 * t + NE]
                for k in range(NB):
                    if t == 0:
                        ready(k)
                    pe.matmul(o, h[:, k, 1 + a:1 + b_], rwt[:, k, :], start=(k == 0), stop=False)
                ins = pe.matmul(o, ones[0:1, 0:b_ - a], rbr[0:1, :], start=False, stop=True)
            ins.then_inc(S("logits"), 1)
            for t, (a, b_) in enumerate(TOK):
                for g in range(2):
                    q = 2 * t + g
                    wait(pe, "tok_ev", q - 1)
                    for j in range(4):
                        ins = pe.transpose(bank[2 + q % 2][0:b_ - a, 128 * j:128 * j + 128],
                                           h[:, 4 * g + j, 1 + a:1 + b_], ident)
                    ins.then_inc(S("tokmajor"), 1)
            pe.wait_ge(S("ranks_in"), 1)
            for t, (a, b_) in enumerate(TOK):
                o = bank[0][0:b_ - a, 64 + 16 * t:64 + 16 * t + NE]
                for t2 in range(t):
                    pe.matmul(o, ones[:, 0:b_ - a], msk[:, t2, :], start=(t2 == 0), stop=False)
                pe.matmul(o, tri[0:b_ - a, 0:b_ - a], msk[0:b_ - a, t, :], start=(t == 0), stop=True)
            for t, (a, b_) in enumerate(TOK):
                ins = pe.matmul(bank[0][:, 128:128 + NE], ones[0:b_ - a, :], msk[0:b_ - a, t, :], start=(t == 0),
                                stop=(t == 2))
            ins.then_inc(S("ranked"), 1)
            pe.wait_ge(S("tok_ev"), 6)

            def gather(j):
                pe.wait_ge(S("sel"), j + 1)
                for g in range(2):
                    for q in range(4):
                        for t, (a, b_) in enumerate(TOK):
                            ins = pe.matmul(bank[4 + g][:, CAP * q:CAP * q + CAP],
                                            htm[0:b_ - a, t, 128 * (4 * g + q):128 * (4 * g + q) + 128],
                                            sel[0:b_ - a, t, :], start=(t == 0), stop=(t == 2))
                    ins.then_inc(S("gath"), 1)

            def down(j, f):
                pe.wait_ge(S("hev"), j * FE + f + 1)
                if f == 0:
                    wait(pe, "scat_ev", j * NB)
                for o in range(2):
                    ins = pe.matmul(bank[2 + o][0:CAP, :], he[:, f, :],
                                    ring3[f][:, 2 * D + 512 * o:2 * D + 512 * o + 512], start=(f == 0),
                                    stop=(f == FE - 1))
                ins.then_inc(S("job"), 1)

            def job(j):
                pe.wait_ge(S("xe_ev"), (j + 1) * 2)
                for f in range(FE):
                    pe.wait_ge(mslot_in[f], (j + 1) * 16)
                    w = ring3[f].rearrange("p (o k c) -> p o k c", o=3, k=NB)
                    if f >= 2:
                        pe.wait_ge(S("hev"), j * FE + f - 1)
                    for o in range(2):
                        for k in range(NB):
                            ins = pe.matmul(bank[f % 2][:, CAP * o:CAP * o + CAP], w[:, o, k, :], h[:, k, 0:CAP],
                                            start=(k == 0), stop=(k == NB - 1))
                    ins.then_inc(S("w13"), 1)
                    if f >= 1:
                        down(j, f - 1)
                down(j, FE - 1)
                gather(j + 1)
                pe.wait_ge(S("selg"), j + 1)
                wait(pe, "scat_ev", j * NB)
                for t, (a, b_) in enumerate(TOK):
                    ins = pe.transpose(bank[7][0:CAP, a:b_], selg[0:b_ - a, t, :], ident[0:b_ - a, 0:b_ - a])
                ins.then_inc(S("sel_t"), 1)
                pe.wait_ge(S("y_ev"), (j + 1) * 2)
                pe.wait_ge(S("selt_ev"), j + 1)
                for n in range(NB):
                    if n >= 4:
                        pe.wait_ge(S("scat_ev"), j * NB + n - 3)
                    pe.matmul(bank[SCAT[n % 4]][:, 0:T], yout[0:CAP, 128 * n:128 * n + 128], selt[0:CAP, :],
                              start=True, stop=True).then_inc(S("scat"), 1)

            gather(0)
            job(0)
            with pe.Fori(1, NE) as j:
                job(j)
            pe.wait_ge(S("joblist"), 1)
            extra = pe.value_load(jobi[0:1, 0:1], min_val=0, max_val=NJ - NE)
            with pe.If(extra > 0):
                with pe.Fori(NE, extra + NE) as j:
                    job(j)
            channel_sum(scr, squares(5))

        @block.scalar
        def _(act):
            A = act.activation

            def taken(key, ins):
                ins.then_inc(pfree[pbank(key)[1]], 1)

            def pcopy(key, out, func=ACT.Copy, rows=128, cols=T, **kw):
                pwait_full(act, key)
                b = pbank(key)[0]
                taken(key, A(out, b[0:rows, 0:cols], func, **kw))

            def ada(n):
                if n >= 28:
                    return
                act.wait_ge(S("ada_mm"), 2 * n + 2)
                wait(act, "ada_tr", n - 1)
                A(arow[0:NC, n % 2, :], bank[6][0:NC, :], ACT.Copy).then_inc(S("ada_row"), 1)

            def norm(i, sums, shift, dst, after=None):
                if i == 5:
                    act.wait_ge(S("x_new"), 1)
                square(after)
                root(i, sums)
                shifted(i, shift, dst)

            tables = [0]

            def table(func):
                wait(act, "table", tables[0])
                tables[0] += 1
                A(tset[:, 1:2], tset[:, 0:1], func).then_inc(S("table"), 1)

            def square(after):
                table(ACT.Sqrt)
                for k in range(NB):
                    if after:
                        pwait_taken(act, (after, k))
                    A(scr[:, k, :], x[:, k, :], ACT.Square).then_inc(S("square"), 1)

            def root(i, sums):
                act.wait_ge(S("norm_sum"), sums)
                A(rtmp, bank[5 if i == 1 else 7][:, 128:128 + T], ACT.Sqrt, bias=eps[:, 0:1], scale=1.0 / D)\
                    .then_inc(S("norm_root"), 1)

            def shifted(i, shift, dst):
                for k in range(NB):
                    act.wait_ge(S("hmul"), (i - 1) * NB + k + 1)
                    A(dst(k)[:, 0:SEQ], dst(k)[:, 0:SEQ], ACT.Identity, bias=mod[:, shift + k, 0:1])\
                        .then_inc(S("hadd"), 1)

            act.wait_ge(S("c_in"), 16)
            A(csil[:, :, :], csil[:, :, :], ACT.Silu).then_inc(S("csil"), 1)
            hk = lambda k: h[:, k, 1:T + 1]
            ada(0)
            act.wait_ge(S("consts"), 1)
            ada(1)
            act.wait_ge(S("x_in"), 16)
            square(None)
            ada(2)
            root(1, 1)
            ada(3)
            shifted(1, 0, hk)
            ada(4)
            ada(5)
            act.wait_ge(S("shb_ready"), 1)
            act.dma_start(io["shift_out"], shb[:, :, :]).then_inc(S("shift_o"), 16)
            pcopy(("lw1", 0), ex[0:64, 0, :], ACT.Tanh, rows=64)
            pwait_full(act, ("la1", 0))
            taken(("la1", 0), A(ex[64:128, 0, :], pbank(("la1", 0))[0][64:128, 0:T], ACT.Copy))
            pcopy(("lg1", 0), tg, ACT.Sigmoid)
            for n in range(NB):
                pcopy(("w", n), lw[:, n, :], ACT.Sigmoid, bias=pc("w0", n))
            for n in range(NB):
                pcopy(("a", n), att[:, n, :], ACT.Sigmoid, bias=pc("a0", n))
            for n in range(NB):
                pcopy(("k", n), ktt[:, n, :])
                if n == 4:
                    act.wait_ge(S("p1_ready"), 1)
                    A(ex[:, :, :], cum[:, :, :], ACT.Exp).then_inc(S("expc"), 1)
                if n == 5:
                    A(lw[:, :, :], lw[:, :, :], ACT.Exp).then_inc(S("expc"), 1)
                if n == 6:
                    A(cum[:, :, :], cum[:, :, :], ACT.Exp, scale=-1.0).then_inc(S("expc"), 1)
            for n in range(4):
                pcopy(("r", n), rt[:, n, :])
            for n in range(NB):
                pcopy(("kks", n), tmp[:, n, :], ACT.Sqrt)
            for n in range(4, NB):
                pcopy(("r", n), rt[:, n, :])
            for n in range(4):
                pcopy(("v", n), vt[:, n, :])
            for n in range(NB):
                pcopy(("bon", n), scr[:, n, :])
            for n in range(4, NB):
                pcopy(("v", n), vt[:, n, :])

            COPY = {"P2": pp_, "P2T": ppt, "P4": p4_, "P4T": p4t, "P8": pp_, "Btm": btm, "Ktm": ktm, "Vtm": vtm,
                    "T4": tt_, "T5": tt_, "W": ww_, "W2": ww_, "X": xst, "SA": sast}
            for step in STEPS:
                if step[0] == "ada":
                    ada(step[1])
                elif step[0] == "g2":
                    for n in range(NB):
                        pcopy(("g2", n), gg[:, n, :])
                elif step[0] == "sample_a":
                    for z in range(2):
                        key = ("smp", 3 * step[1] + z)
                        pcopy(key, (sq1, sq2)[z].rearrange("p a b -> p (a b)"), cols=512)
                elif step[0] == "prod":
                    _, c, nm = step
                    if nm in COPY or nm == "Y":
                        b, i, u = gbank(c, nm)
                        act.wait_ge(cfull[i], u)
                        dst = yy[:, :, C * c:C * c + C] if nm == "Y" else COPY[nm]
                        dst = dst[c % 2] if isinstance(dst, list) else dst
                        A(dst[:, :, :], b.rearrange("p (a b) -> p a b", a=NB), ACT.Copy).then_inc(S("e_" + nm), 1)
            act.wait_ge(S("e_S0"), NCH + 1)
            act.dma_start(io["wkv_out"], s0st[:, :, :]).then_inc(S("wkv_o"), 16)
            table(ACT.Sqrt)
            for n in range(NB):
                pwait_taken(act, ("gnm", n))
                A(scr2[:, n, :], yy[:, n, :], ACT.Square).then_inc(S("gn_square"), 1)
            act.wait_ge(S("gn_sum"), 1)
            A(gsd[0:16, :], bank[6][0:16, 0:T], ACT.Sqrt, bias=eps[0:16, 1:2], scale=1.0 / C).then_inc(S("gn_root"), 1)
            norm(2, 2, 24, hk, "wo")
            for n in range(NF):
                wait(act, "ff_h", n - 1)
                pcopy(("up", n), glf[:, n % 2, :], ACT.Silu)
            norm(3, 3, 48, hk, "down")
            for n in range(NB):
                act.wait_ge(S("glu_mm"), n + 1)
                if n >= 2:
                    pwait_taken(act, ("pw1", n - 2))
                A(gl[:, n % 2, :], bank[4 + n % 2][:, 0:T], ACT.Sigmoid, bias=pc("pw1_b", NB + n))\
                    .then_inc(S("glu_gate"), 1)
            pwait_taken(act, ("pw1", NB - 1))
            act.dma_start(io["convp"], upad[:, :, SEQ:SEQ + CW - 1]).then_inc(S("conv_o"), 16)
            act.dma_start(io["convs"], cbuf[:, :, 1:CW]).then_inc(S("conv_o"), 16)
            table(ACT.Sqrt)
            for m in range(NB - NV):
                act.wait_ge(S("conv_mm"), m + 1)
                A(zz[:, NV + m, 0:SEQ], bank[2 + m][:, 0:SEQ], ACT.Identity, bias=pc("dw_b", NV + m))\
                    .then_inc(S("conv_ev"), 1)
            act.wait_ge(S("norm_sum"), 4)
            A(rtmp, bank[7][:, 128:128 + T], ACT.Copy, scale=1.0 / D).then_inc(S("ln_mean"), 1)
            for n in range(NB):
                act.wait_ge(S("ln_centered"), n + 1)
                A(scr[:, n, :], zz[:, n, :], ACT.Square).then_inc(S("ln_square"), 1)
            act.wait_ge(S("norm_sum"), 5)
            A(rtmp, bank[7][:, 128:128 + T], ACT.Sqrt, bias=eps[:, 2:3], scale=1.0 / D).then_inc(S("ln_root"), 1)
            for n in range(NB):
                act.wait_ge(S("ln_scaled"), n + 1)
                A(zz[:, n, :], zz[:, n, :], ACT.Silu, bias=pc("ln_b", n), scale=pc("ln_g", n))\
                    .then_inc(S("z_ready"), 1)
            norm(4, 6, 72, hk, "pw2")
            act.wait_ge(S("conv_o"), 32)
            for t, (a, b_) in enumerate(TOK):
                for g in range(2):
                    act.wait_ge(S("tokmajor"), 2 * t + g + 1)
                    A(htm[0:b_ - a, t, 512 * g:512 * g + 512], bank[2 + g][0:b_ - a, :], ACT.Copy)\
                        .then_inc(S("tok_ev"), 1)
            table(ACT.Exp)
            act.wait_ge(S("diff"), 1)
            A(mx[:, 3:6], mx[:, 3:6], ACT.Exp).then_inc(S("ediff"), 1)

            def gathered(j):
                for g in range(2):
                    act.wait_ge(S("gath"), j * 2 + g + 1)
                    A(h[:, 4 * g:4 * g + 4, 0:CAP], bank[4 + g][:, 0:4 * CAP].rearrange("p (a b) -> p a b", a=4),
                      ACT.Copy).then_inc(S("xe_ev"), 1)

            def job(j):
                for f in range(FE):
                    act.wait_ge(S("w13"), j * FE + f + 1)
                    if f >= 2:
                        act.wait_ge(S("hev"), j * FE + f - 1)
                    else:
                        wait(act, "hev", j * FE + f - 1)
                    A(silm[:, f % 2, :], bank[f % 2][:, 0:CAP], ACT.Silu).then_inc(S("sil"), 1)
                act.wait_ge(S("job"), (j + 1) * FE)
                wait(act, "scat", j * NB)
                for o in range(2):
                    A(yout[0:CAP, 512 * o:512 * o + 512], bank[2 + o][0:CAP, :], ACT.Copy).then_inc(S("y_ev"), 1)
                gathered(j + 1)
                act.wait_ge(S("sel_t"), j + 1)
                A(selt[0:CAP, :], bank[7][0:CAP, 0:T], ACT.Copy).then_inc(S("selt_ev"), 1)

            gathered(0)
            job(0)
            with act.Fori(1, NE) as j:
                job(j)
            act.wait_ge(S("joblist"), 1)
            extra = act.value_load(jobi[0:1, 0:1], min_val=0, max_val=NJ - NE)
            with act.If(extra > 0):
                with act.Fori(NE, extra + NE) as j:
                    job(j)
            norm(5, 7, 96, lambda k: scr[:, k, :])

        @block.vector
        def _(dve):
            chain = [0]

            def link(ins):
                chain[0] += 1
                ins.then_inc(S("dve_chain"), 1)
                dve.wait_ge(S("dve_chain"), chain[0])

            TT, TS, STT = dve.tensor_tensor, dve.tensor_scalar, dve.scalar_tensor_tensor

            def bc(v, n):
                return v.unsqueeze(2).to_broadcast([v.shape[0], v.shape[1], n])

            def mid(v, n):
                return v.unsqueeze(1).to_broadcast([v.shape[0], n, v.shape[1]])

            def ada(n):
                if n:
                    m = n - 1
                    dve.wait_ge(S("ada_tr"), m + 1)
                    o = (m % 2) * 4 * NC
                    TT(mod[:, 4 * m:4 * m + 4, :], bank[7][:, o:o + 4 * NC].rearrange("p (a b) -> p a b", a=4),
                       bc(adab[:, 4 * m:4 * m + 4], NC), ALU.add).then_inc(S("ada_ev"), 1)

            adab = par[:, PCOL["ada_b"]:PCOL["ada_b"] + 112]

            def norm(i, shift, scale, g, dst, wide):
                dve.wait_ge(S("ada_ev"), 4 if i == 1 else 28)
                link(STT(gain[:, :, :], mod[:, scale:scale + NB, :], 1.0, bc(g, NC), ALU.add, ALU.mult))
                link(TT(smt[:, 0, :, :], x[:, :, SEQ:T], gain[:, :, 1:NC], ALU.mult))
                if i > 1:
                    dve.wait_ge(S("norm_root"), i)
                    link(dve.reciprocal(rstd, rtmp))
                for k in range(NB):
                    STT(dst(k)[:, 0:SEQ], x[:, k, 0:SEQ], gain[:, k, 0:1], rstd[:, 0:SEQ], ALU.mult, ALU.mult)\
                        .then_inc(S("hmul"), 1)
                    if k == 0:
                        ins = TT(smt[:, 1, :, :], smt[:, 0, :, :], mid(rstd[:, SEQ:T], NB), ALU.mult)
                        ins.then_inc(S("hscaled"), 1)
                    if k == 1:
                        dve.wait_ge(S("hscaled"), i)
                        TT(wide, smt[:, 1, :, :], mod[:, shift:shift + NB, 1:NC], ALU.add).then_inc(S("hsamp"), 1)

            def residual(b, n, gate, done, bias=None):
                g0, gs = mod[:, gate + n, 0:1], mod[:, gate + n, 1:NC]
                if bias is None:
                    STT(x[:, n, 0:SEQ], b[:, 0:SEQ], g0, x[:, n, 0:SEQ], ALU.mult, ALU.add)
                    link(TT(smt[:, 0, n, :], b[:, SEQ:T], gs, ALU.mult))
                else:
                    TS(scr[:, n, 0:SEQ], b[:, 0:SEQ], bias, g0, ALU.add, ALU.mult)
                    link(STT(smt[:, 0, n, :], b[:, SEQ:T], bias, gs, ALU.add, ALU.mult))
                    TT(x[:, n, 0:SEQ], scr[:, n, 0:SEQ], x[:, n, 0:SEQ], ALU.add)
                done(TT(x[:, n, SEQ:T], smt[:, 0, n, :], x[:, n, SEQ:T], ALU.add))

            def taken(key):
                return lambda ins: ins.then_inc(pfree[pbank(key)[1]], 1)

            dve.wait_ge(S("consts"), 1)
            dve.memset(eps[:, 0:1], RMS_EPS)
            dve.memset(eps[:, 1:2], GN_EPS)
            dve.memset(eps[:, 2:3], LN_EPS)
            dve.memset(h[:, :, 0:1], 0.0)
            dve.wait_ge(S("par_in"), 16)
            for n in range(4):
                ada(n)
            dve.wait_ge(S("x_in"), 16)
            dve.wait_ge(S("norm_root"), 1)
            link(dve.reciprocal(rstd, rtmp))
            ada(4)
            norm(1, 0, 8, pc("norm_mix_g", 0, NB), lambda k: h[:, k, 1:T + 1], h[:, :, SEQ + 1:T + 1])
            dve.wait_ge(S("hadd"), NB)
            dve.wait_ge(S("shift_in"), 16)
            TT(xx[:, :, 0:SEQ], h[:, :, 0:SEQ], h[:, :, 1:SEQ + 1], ALU.subtract)
            TT(xx[:, :, SEQ:T], shf[:, :, :], h[:, :, SEQ + 1:T + 1], ALU.subtract).then_inc(S("xx"), 1)
            dve.wait_ge(S("xx"), 1)
            dve.tensor_copy(shb[:, :, :], h[:, :, SEQ:T + 1]).then_inc(S("shb_ready"), 1)

            def mixture(q, m, after):
                if after:
                    pwait_full(dve, after)
                for k in range(NB):
                    ins = STT(xi[q % 2][:, k, :], xx[:, k, :], pc("mu", m * NB + k), h[:, k, 1:T + 1],
                              ALU.mult, ALU.add)
                ins.then_inc(S("xi"), 1)

            mixture(0, 1, None)
            mixture(1, 4, None)
            ada(5)
            mixture(2, 5, ("lw1", 0))
            mixture(3, 2, ("la1", 0))
            mixture(4, 0, ("lg1", 0))
            dve.wait_ge(S("masks"), 1)
            pwait_taken(dve, ("w", NB - 1))
            link(TS(lw[:, :, :], lw[:, :, :], DECAY, None, ALU.mult))
            for n in range(NB):
                ins = dve.tensor_tensor_scan(cum[:, n, :], scanm, lw[:, n, :], 0.0, ALU.mult, ALU.add)
            link(ins)
            TT(lw[:, :, :], cum[:, :, :], lw[:, :, :], ALU.subtract).then_inc(S("p1_ready"), 1)
            pwait_taken(dve, ("k", NB - 1))
            pwait_taken(dve, ("k", NB - 2))
            link(TT(btt[:, :, :], ktt[:, :, :], bc(pc("kk", 0, NB), T), ALU.mult))
            TT(scr[:, :, :], btt[:, :, :], btt[:, :, :], ALU.mult).then_inc(S("kk_sq"), 1)
            mixture(5, 3, ("k", NB - 1))
            dve.wait_ge(S("xi"), 6)
            link(TS(xx[:, :, :], att[:, :, :], -1.0, None, ALU.add))
            link(TT(xx[:, :, :], xx[:, :, :], bc(pc("ka", 0, NB), T), ALU.mult))
            link(STT(ktt[:, :, :], xx[:, :, :], 1.0, ktt[:, :, :], ALU.add, ALU.mult))
            pwait_taken(dve, ("kks", NB - 1))
            pwait_taken(dve, ("kks", NB - 2))
            link(TS(tmp[:, :, :], tmp[:, :, :], 1e-12, None, ALU.max))
            link(dve.reciprocal(tmp[:, :, :], tmp[:, :, :]))
            link(STT(btt[:, :, :], btt[:, :, :], -1.0, tmp[:, :, :], ALU.mult, ALU.mult))
            link(STT(att[:, :, :], btt[:, :, :], -1.0, att[:, :, :], ALU.mult, ALU.mult))
            pwait_taken(dve, ("r", NB - 1))
            pwait_taken(dve, ("r", NB - 2))
            link(TT(tmp[:, :, :], rt[:, :, :], ktt[:, :, :], ALU.mult))
            TT(tmp[:, :, :], tmp[:, :, :], bc(pc("rk", 0, NB), T), ALU.mult).then_inc(S("rk_prod"), 1)
            dve.wait_ge(S("expc"), 3)
            for k, v in enumerate((rt, ex, ktt, None, btt, att)):
                if v is not None:
                    ins = dve.tensor_copy(smp[:, k * NB:(k + 1) * NB, :], v[:, :, SEQ:T])
            link(ins)
            TT(rt[:, :, :], rt[:, :, :], ex[:, :, :], ALU.mult)
            TT(btt[:, :, :], btt[:, :, :], lw[:, :, :], ALU.mult)
            TT(att[:, :, :], att[:, :, :], cum[:, :, :], ALU.mult)
            TT(ktt[:, :, :], ktt[:, :, :], cum[:, :, :], ALU.mult)
            for c in range(NCH):
                dve.tensor_copy(ecl[:, :, c:c + 1], ex[:, :, C * c + C - 1:C * c + C])
            dve.memset(s0st[:, :, :], 0.0).then_inc(S("e_S0"), 1)
            pwait_taken(dve, ("v", NB - 1))
            pwait_taken(dve, ("v", NB - 2))
            dve.tensor_copy(smp[:, 3 * NB:4 * NB, :], vt[:, :, SEQ:T]).then_inc(S("zeros"), 1)
            link(TT(bonus[:, :, :], scr[:, :, :], vt[:, :, :], ALU.mult))
            TT(bonus[:, :, :], bonus[:, :, :], bc(pc("lnx_b", 0, NB), T), ALU.add)
            MASK = {"M": [(p_, m_p, "P")], "MT": [(pt_, m_pt, "PT"), (m32, m_32t, "M32"), (m64, m_64t, "M64")],
                    "NT": [(nt, m_su, "NT")], "QBT": [(qbt, m_iu, "QBT")], "QKT": [(qkt, m_iu, "QKT")]}
            for step in STEPS:
                if step[0] == "ada":
                    ada(step[1])
                elif step[0] == "sample_b":
                    hp = step[1]
                    key = ("smp", 3 * hp + 2)
                    pwait_full(dve, key)
                    v = TT(sq3[:, :, :], pbank(key)[0].rearrange("p (a b) -> p a b", a=NS), mid(id64, NS), ALU.mult)
                    taken(key)(v)
                    pwait_taken(dve, key)
                    dve.tensor_reduce(yy[:, hp, SEQ:T], sq3[:, :, :], AX, ALU.add).then_inc(S("s_fold"), 1)
                elif step[0] == "prod":
                    _, c, nm = step
                    b, i, u = gbank(c, nm)
                    bv = b.rearrange("p (a b) -> p a b", a=NB)
                    if nm in MASK:
                        dve.wait_ge(cfull[i], u)
                        for dst, m, name in MASK[nm]:
                            dst = dst[c % 2] if isinstance(dst, list) else dst
                            TT(dst[:, :, :], bv, mid(m[:, 0:C], NB), ALU.mult).then_inc(S("e_" + name), 1)
                        if nm == "MT":
                            dve.wait_ge(S("e_PT"), c + 1)
                            TT(uu[c % 2][:, :, :], pt_[:, :, :], mid(id64, NB), ALU.add).then_inc(S("e_U1"), 1)
                    elif nm[0] == "U":
                        dve.wait_ge(S("e_U" + str(int(nm[1]) - 1)), c + 1)
                        dve.wait_ge(cfull[i], u)
                        TT(uu[c % 2][:, :, :], bv, uu[c % 2][:, :, :], ALU.add).then_inc(S("e_" + nm), 1)
                    elif nm == "S":
                        dve.wait_ge(cfull[i], u)
                        link(TT(s0st[:, :, :], bv, s0st[:, :, :], ALU.add))
                        TT(s0st[:, :, :], s0st[:, :, :], ecl[:, :, c:c + 1].to_broadcast([128, NB, C]), ALU.mult)\
                            .then_inc(S("e_S0"), 1)
                        dve.wait_ge(S("e_S0"), c + 2)
            dve.wait_ge(S("e_Y"), NCH)
            dve.wait_ge(S("s_fold"), NB)
            dve.wait_ge(S("ada_ev"), 28)
            for n in range(NB):
                pwait_full(dve, ("gnm", n))
                taken(("gnm", n))(STT(yy[:, n, :], pbank(("gnm", n))[0][:, 0:T], -1.0 / C, yy[:, n, :],
                                      ALU.mult, ALU.add))
            dve.wait_ge(S("gn_root"), 1)
            dve.reciprocal(gsd[0:16, :], gsd[0:16, :]).then_inc(S("gn_rstd"), 1)
            for n in range(NB + 2):
                if n < NB:
                    pwait_full(dve, ("gnb", n))
                    taken(("gnb", n))(TT(yy[:, n, :], pbank(("gnb", n))[0][:, 0:T], yy[:, n, :], ALU.mult))
                if 1 <= n <= NB:
                    pwait_taken(dve, ("gnb", n - 1))
                    STT(oo[:, n - 1, :], yy[:, n - 1, :], pc("lnx_g", n - 1), bonus[:, n - 1, :], ALU.mult, ALU.add)\
                        .then_inc(S("gn_mid"), 1)
                if n >= 2:
                    if n == 2:
                        pwait_taken(dve, ("g2", NB - 1))
                        pwait_taken(dve, ("g2", NB - 2))
                    dve.wait_ge(S("gn_mid"), n - 1)
                    TT(oo[:, n - 2, :], oo[:, n - 2, :], gg[:, n - 2, :], ALU.mult).then_inc(S("gn_out"), 1)
            for n in range(NB):
                pwait_full(dve, ("wo", n))
                residual(pbank(("wo", n))[0], n, 16, taken(("wo", n)))

            def x_done():
                dve.tensor_copy(eps[:, 3:4], x[:, NB - 1, T - 1:T]).then_inc(S("x_new"), 1)

            pwait_taken(dve, ("wo", NB - 1))
            pwait_taken(dve, ("wo", NB - 2))
            norm(2, 24, 32, pc("norm_ffn_g", 0, NB), lambda k: h[:, k, 1:T + 1], h[:, :, SEQ + 1:T + 1])
            for n in range(NF):
                pwait_taken(dve, ("up", n))
                dve.wait_ge(S("ff_up"), n + 1)
                TT(ff[:, n, :], bank[4 + n % 2][:, 0:T], glf[:, n % 2, :], ALU.mult).then_inc(S("ff_h"), 1)
            for n in range(NB):
                pwait_full(dve, ("down", n))
                residual(pbank(("down", n))[0], n, 40, taken(("down", n)))
            pwait_taken(dve, ("down", NB - 1))
            pwait_taken(dve, ("down", NB - 2))
            norm(3, 48, 56, pc("norm_mix_g", NB, NB), lambda k: h[:, k, 1:T + 1], h[:, :, SEQ + 1:T + 1])
            dve.wait_ge(S("s_out"), 16 * NB)
            dve.wait_ge(S("wkv_o"), 16)
            dve.memset(upad[:, :, 0:CW - 1], 0.0)
            dve.wait_ge(S("conv_in"), 16)
            dwp = par[:, PCOL["dw"]:PCOL["dw"] + NB * CW].rearrange("p (n w) -> p n w", n=NB)
            taps = TAPS_V
            done = [0]

            def convolve(upto):
                for k in range(done[0], upto):
                    n, w = taps[k]
                    if w == 0:
                        pwait_taken(dve, ("pw1", n))
                        ins = TS(zz[:, n, 0:SEQ], upad[:, n, 0:SEQ], dwp[:, n, 0:1], pc("dw_b", n), ALU.mult, ALU.add)
                    else:
                        dve.wait_ge(S("tap"), TAP_AT[n, w - 1] + 1)
                        ins = STT(zz[:, n, 0:SEQ], upad[:, n, w:w + SEQ], dwp[:, n, w:w + 1], zz[:, n, 0:SEQ],
                                  ALU.mult, ALU.add)
                    ins.then_inc(S("tap"), 1)
                done[0] = upto

            for n in range(NB):
                dve.wait_ge(S("glu_gate"), n + 1)
                pwait_full(dve, ("pw1", n))
                b = pbank(("pw1", n))[0]
                STT(upad[:, n, CW - 1:CW - 1 + SEQ], b[:, 0:SEQ], pc("pw1_b", n), gl[:, n % 2, 0:SEQ], ALU.add, ALU.mult)
                taken(("pw1", n))(STT(cbuf[:, n * NS:(n + 1) * NS, CW - 1], b[:, SEQ:T], pc("pw1_b", n),
                                      gl[:, n % 2, SEQ:T], ALU.add, ALU.mult))
                there = [k for k, (m, w) in enumerate(taps) if m > n] + [len(taps)]
                convolve(max(done[0], min(there[0], TAPS * (n - NG + 1))))
            pwait_taken(dve, ("pw1", NB - 1))
            link(TT(cprd.rearrange("p (n b) w -> p n b w", n=NB), cbuf.rearrange("p (n b) w -> p n b w", n=NB),
                    dwp.unsqueeze(2).to_broadcast([128, NB, NS, CW]), ALU.mult))
            link(dve.tensor_reduce(smt[:, 0, :, :].rearrange("p a b -> p (a b)"), cprd[:, :, :], AX, ALU.add))
            TT(zz[:, :, SEQ:T], smt[:, 0, :, :], bc(pc("dw_b", 0, NB), NS), ALU.add).then_inc(S("conv_done"), 1)
            convolve(len(taps))
            dve.wait_ge(S("ln_mean"), 1)
            dve.wait_ge(S("conv_done"), 1)
            dve.wait_ge(S("tap"), len(taps))
            dve.wait_ge(S("conv_ev"), NB - NV)
            dve.wait_ge(S("tap_g"), NG * CW)
            for n in range(NB):
                TT(zz[:, n, :], zz[:, n, :], rtmp, ALU.subtract).then_inc(S("ln_centered"), 1)
            dve.wait_ge(S("ln_root"), 1)
            dve.wait_ge(S("ln_centered"), NB)
            link(dve.reciprocal(rstd, rtmp))
            for n in range(NB):
                TT(zz[:, n, :], zz[:, n, :], rstd, ALU.mult).then_inc(S("ln_scaled"), 1)
            for n in range(NB):
                pwait_full(dve, ("pw2", n))
                residual(pbank(("pw2", n))[0], n, 64, taken(("pw2", n)), bias=pc("pw2_b", n))
            pwait_taken(dve, ("pw2", NB - 1))
            pwait_taken(dve, ("pw2", NB - 2))
            norm(4, 72, 80, pc("norm_ffn_g", NB, NB), lambda k: h[:, k, 1:T + 1], h[:, :, SEQ + 1:T + 1])

            link(dve.memset(lg[:, :, :], 0.0))
            dve.wait_ge(S("logits"), 1)
            b0 = bank[0][:, 0:48].rearrange("p (t e) -> p t e", t=3)
            dve.tensor_copy(lg[:, 0:2, :], b0[:, 0:2, 0:NE])
            link(dve.tensor_copy(lg[0:NS, 2:3, :], b0[0:NS, 2:3, 0:NE]))

            def best(src, m, oh):
                link(dve.tensor_reduce(m, src[:, :, :], AX, ALU.max))
                link(TT(sc1[:, :, :], src[:, :, :], bc(m, NE), ALU.is_equal))
                link(TT(sc1[:, :, :], sc1[:, :, :], mid(iota_e, 3), ALU.mult))
                link(dve.tensor_reduce(cur[:, 0:3], sc1[:, :, :], AX, ALU.max))
                link(TT(oh[:, :, :], sc1[:, :, :], bc(cur[:, 0:3], NE), ALU.is_equal))

            best(lg, mx[:, 0:3], oh1)
            link(STT(sc2[:, :, :], oh1[:, :, :], -3e38, lg[:, :, :], ALU.mult, ALU.add))
            best(sc2, mx[:, 3:6], oh2)
            TT(msk[:, :, :], oh1[:, :, :], oh2[:, :, :], ALU.add).then_inc(S("ranks_in"), 1)
            TT(mx[:, 3:6], mx[:, 3:6], mx[:, 0:3], ALU.subtract).then_inc(S("diff"), 1)
            dve.memset(jg[:, :, :], 0.0)
            dve.memset(jr[:, :, :], -BIG)
            link(dve.memset(sc2[:, :, :], 0.0))
            dve.wait_ge(S("ranked"), 1)
            rk = bank[0][:, 64:112].rearrange("p (t e) -> p t e", t=3)
            dve.tensor_copy(sc2[:, 0:2, :], rk[:, 0:2, 0:NE])
            dve.tensor_copy(cnt, bank[0][:, 128:128 + NE])
            link(dve.tensor_copy(sc2[0:NS, 2:3, :], rk[0:NS, 2:3, 0:NE]))
            link(STT(sc1[:, :, :], sc2[:, :, :], BIG, msk[:, :, :], ALU.add, ALU.mult))
            link(TS(jr[:, :, 0:NE], sc1[:, :, :], -BIG, None, ALU.add))

            def pick(j):
                dve.tensor_copy(cur[:, 0:3].unsqueeze(2), jr[:, :, bass.ds(j, 1)]).then_inc(S("curr"), 1)
                dve.wait_ge(S("curr"), j + 1)
                for t in range(3):
                    ins = TS(sel[:, t, :], iota_c, cur[:, t:t + 1], None, ALU.is_equal)
                ins.then_inc(S("sel"), 1)

            pick(0)
            dve.wait_ge(S("ediff"), 1)
            link(TS(mx[:, 0:3], mx[:, 3:6], 1.0, None, ALU.add))
            link(dve.reciprocal(mx[:, 0:3], mx[:, 0:3]))
            link(TT(mx[:, 3:6], mx[:, 0:3], mx[:, 3:6], ALU.mult))
            link(TT(oh1[:, :, :], oh1[:, :, :], bc(mx[:, 0:3], NE), ALU.mult))
            link(TT(oh2[:, :, :], oh2[:, :, :], bc(mx[:, 3:6], NE), ALU.mult))
            link(TT(jg[:, :, 0:NE], oh1[:, :, :], oh2[:, :, :], ALU.add))
            for k in range(2):
                TS(rx[:, :, NE * k:NE * k + NE], sc1[:, :, :], -float(CAP * (k + 1)), None, ALU.add)
                dve.tensor_copy(gx[:, :, NE * k:NE * k + NE], jg[:, :, 0:NE])
                ins = TS(flg[:, NE * k:NE * k + NE], cnt, float(CAP * (k + 1)), None, ALU.is_gt)
            link(ins)
            link(dve.tensor_tensor_scan(pos, ones[:, 0:16], flg, 0.0, ALU.mult, ALU.add))
            for m in range(NJ - NE):
                link(STT(jm, pos, float(m + 1), flg, ALU.is_equal, ALU.mult))
                link(TT(jt[:, :, :], rx[:, :, :], mid(jm, 3), ALU.mult))
                link(dve.tensor_reduce(cur[:, 3:6], jt[:, :, :], AX, ALU.add))
                TS(jr[:, :, NE + m], cur[:, 3:6], -BIG, None, ALU.add)
                link(TT(jt[:, :, :], gx[:, :, :], mid(jm, 3), ALU.mult))
                dve.tensor_reduce(jg[:, :, NE + m], jt[:, :, :], AX, ALU.add)
                link(TT(jm, jm, eidx, ALU.mult))
                link(dve.tensor_reduce(jobf[:, m + 1:m + 2], jm, AX, ALU.add))
            link(dve.tensor_copy(jobf[:, 0:1], pos[:, 15:16]))
            dve.tensor_copy(jobi[0:1, 0:NJ - NE + 1], jobf[0:1, 0:NJ - NE + 1]).then_inc(S("joblist"), 1)
            dve.wait_ge(S("joblist"), 1)

            def job(j):
                dve.tensor_copy(cur[:, 3:6].unsqueeze(2), jg[:, :, bass.ds(j, 1)]).then_inc(S("curg"), 1)
                dve.wait_ge(S("curg"), j + 1)
                wait(dve, "sel_t", j)
                for t in range(3):
                    ins = TS(selg[:, t, :], iota_c, cur[:, t:t + 1], cur[:, 3 + t:4 + t], ALU.is_equal, ALU.mult)
                ins.then_inc(S("selg"), 1)
                dve.wait_ge(S("gath"), 2 * j + 2)
                dve.wait_ge(S("selg"), j + 1)
                pick(j + 1)
                for f in range(FE):
                    dve.wait_ge(S("sil"), j * FE + f + 1)
                    TT(he[:, f, :], bank[f % 2][:, CAP:2 * CAP], silm[:, f % 2, :], ALU.mult).then_inc(S("hev"), 1)
                for n in range(NB):
                    dve.wait_ge(S("scat"), j * NB + n + 1)
                    b = bank[SCAT[n % 4]]
                    STT(x[:, n, 0:SEQ], b[:, 0:SEQ], mod[:, 88 + n, 0:1], x[:, n, 0:SEQ], ALU.mult, ALU.add)
                    TT(smt[:, 0, n, :], b[:, SEQ:T], mod[:, 88 + n, 1:NC], ALU.mult).then_inc(S("scat_ev"), 1)
                dve.wait_ge(S("scat_ev"), j * NB + NB)
                TT(x[:, :, SEQ:T], smt[:, 0, :, :], x[:, :, SEQ:T], ALU.add).then_inc(S("x_job"), 1)
                dve.wait_ge(S("x_job"), j + 1)

            job(0)
            with dve.Fori(1, NE) as j:
                job(j)
            extra = dve.value_load(jobi[0:1, 0:1], min_val=0, max_val=NJ - NE)
            with dve.If(extra > 0):
                with dve.Fori(NE, extra + NE) as j:
                    job(j)
            x_done()
            norm(5, 96, 104, pc("final_g", 0, NB), lambda k: scr[:, k, :], scr[:, :, SEQ:T])

        @block.gpsimd
        def _(pool):
            chain = [0]

            def link(ins):
                chain[0] += 1
                ins.then_inc(S("pool_chain"), 1)
                pool.wait_ge(S("pool_chain"), chain[0])

            AS = pool.affine_select

            def where(out, src, base_, step, cm, op=ALU.is_ge, fill=0.0):
                pat = [[step, out.shape[1]]] if isinstance(step, int) else step
                link(AS(out=out, in_=src, compare_op=op, fill=fill, base=base_, pattern=pat, channel_multiplier=cm))

            pool.memset(ones, 1.0)
            pool.memset(tset, 1.0)
            link(pool.memset(ident, 0.0))
            where(ident, ident, 0, -1, 1, ALU.not_equal, 1.0)
            pool.memset(shb[:, 0, 0:1], 0.0).then_inc(S("consts"), 1)
            pool.memset(bdones, 0.0)
            pool.memset(m_iu, 1.0)
            link(pool.memset(scanm, 1.0))
            for q in range(2):
                link(pool.memset(bdones[64 * q:64 * q + 64, 64 * q:64 * q + 64], 1.0))
            for c in range(NCH):
                pool.memset(scanm[:, C * c:C * c + 1], 0.0)
            link(pool.memset(scanm[:, SEQ:T], 0.0))
            where(tri, ones, -1, 1, -1)
            for q in range(2):
                p = slice(64 * q, 64 * q + 64)
                where(m_iu[p, :], m_iu[p, :], 0, 1, -1)
                link(pool.tensor_copy(id64[p, :], ident[p, 64 * q:64 * q + 64]))
            for m, w in ((m_pt, 16), (m_32t, 32)):
                v = m.rearrange("p (a b) -> p a b", b=w)
                o = ones.rearrange("p (a b) -> p a b", b=w)
                link(AS(out=v, in_=o, compare_op=ALU.is_ge, fill=0.0, base=0, pattern=[[-w, 128 // w], [0, w]],
                        channel_multiplier=1))
                link(AS(out=v, in_=v, compare_op=ALU.is_ge, fill=0.0, base=w - 1, pattern=[[w, 128 // w], [0, w]],
                        channel_multiplier=-1))
            where(m_p, m_pt, -1, -1, 1)
            where(m_pt, m_pt, -1, 1, -1)
            where(m_32t, m_32t, -1, 1, -1)
            where(m_su, bdones, -1, 1, -1)
            link(pool.tensor_tensor(m_64t, m_su, m_32t, ALU.subtract))
            link(pool.tensor_tensor(m_32t, m_32t, m_pt, ALU.subtract))
            for m in (m_su, m_p, m_pt, m_32t, m_64t):
                ins = pool.tensor_copy(m[64:128, 0:C], m[64:128, C:2 * C])
            link(ins)
            pool.iota(iota_c, pattern=[[1, CAP]], base=0, channel_multiplier=0, allow_small_or_imprecise_dtypes=True)
            pool.iota(iota_e, pattern=[[-1, NE]], base=NE, channel_multiplier=0, allow_small_or_imprecise_dtypes=True)
            pool.iota(eidx, pattern=[[0, 2], [1, NE]], base=0, channel_multiplier=0,
                      allow_small_or_imprecise_dtypes=True).then_inc(S("masks"), 1)
            pool.wait_ge(S("masks"), 1)

            pool.wait_ge(S("zeros"), 1)
            TTp = pool.tensor_tensor

            def vec(k, hp):
                return smp[:, k * NB + hp, :].unsqueeze(2).to_broadcast([128, NS, C])

            def load(hp):
                if hp >= 2:
                    pool.wait_ge(S("s_out"), 16 * (hp - 1))
                pool.dma_start(sst[hp % 2][:, :, :], io["state"][hp]).then_inc(S("s_in"), 16)

            def terms(hp):
                s = sst[hp % 2]
                pool.wait_ge(S("s_in"), 16 * (hp + 1))
                if hp:
                    pwait_full(pool, ("smp", 3 * hp - 1))
                TTp(sq1[:, :, :], s[:, :, :], vec(4, hp), ALU.mult).then_inc(S("s_terms"), 1)
                TTp(sq2[:, :, :], id64.unsqueeze(1).to_broadcast([128, NS, C]), vec(3, hp), ALU.mult)\
                    .then_inc(S("s_terms"), 1)

            load(0)
            terms(0)
            link(pool.memset(hrep[0:16, :, :], 1.0))
            for out, src, cm, step in ((hsum, ones.rearrange("p (a b) -> p a b", a=NB), 1, [[128, NB], [-C, 16]]),
                                       (hrep[0:16, :, :], hrep[0:16, :, :], -C, [[128, NB], [1, 128]])):
                link(AS(out=out, in_=src, compare_op=ALU.is_ge, fill=0.0, base=0, pattern=step, channel_multiplier=cm))
                ins = AS(out=out, in_=out, compare_op=ALU.is_ge, fill=0.0, base=C - 1,
                         pattern=[[-a, b] for a, b in step], channel_multiplier=-cm)
                if cm > 0:
                    link(ins)
            ins.then_inc(S("heads_ready"), 1)
            for step in STEPS:
                if step[0] == "sample_a":
                    hp = step[1]
                    s = sst[hp % 2]
                    if hp + 1 < NB:
                        load(hp + 1)
                    pwait_taken(pool, ("smp", 3 * hp))
                    pwait_taken(pool, ("smp", 3 * hp + 1))
                    TTp(sq1[:, :, :], sq1[:, :, :], vec(5, hp), ALU.mult)
                    TTp(sq2[:, :, :], sq2[:, :, :], vec(2, hp), ALU.mult)
                    link(TTp(s[:, :, :], s[:, :, :], vec(1, hp), ALU.mult))
                    link(TTp(s[:, :, :], s[:, :, :], sq1[:, :, :], ALU.add))
                    link(TTp(s[:, :, :], s[:, :, :], sq2[:, :, :], ALU.add))
                    if hp:
                        pool.wait_ge(S("s_fold"), hp)
                    TTp(sq3[:, :, :], s[:, :, :], vec(0, hp), ALU.mult).then_inc(S("s_read"), 1)
                    pool.dma_start(io["state_out"][hp], s[:, :, :]).then_inc(S("s_out"), 16)
                    if hp + 1 < NB:
                        terms(hp + 1)
            pwait_full(pool, ("down", NB - 1))
            pdw = par[:, PCOL["dw"]:PCOL["dw"] + NB * CW]
            for q, end in zip(DIAGS, DIAGS[1:] + [CW * (NB - NV)]):
                for a, e in ((q, min(end, q - q % NDG + NDG)), (q - q % NDG + NDG, end)):
                    if a < e:
                        if a >= NDG:
                            pool.wait_ge(S("conv_mm"), (e - 1 - NDG) // CW + 1)
                        n = e - a
                        ins = TTp(diag[:, a % NDG:a % NDG + n, :], ident.unsqueeze(1).to_broadcast([128, n, 128]),
                                  pdw[:, NV * CW + a:NV * CW + e].unsqueeze(2).to_broadcast([128, n, 128]), ALU.mult)
                ins.then_inc(S("diag"), 1)
                if q == DIAGS[0]:
                    for n in range(NG):
                        pwait_taken(pool, ("pw1", n))
                        for w in range(CW):
                            k = n * CW + w
                            if k >= 2:
                                pool.wait_ge(S("tap_g"), k - 1)
                            pool.tensor_scalar(gtap[:, k % 2, :], upad[:, n, w:w + SEQ], pc("dw", k),
                                               pc("dw_b", n) if w == 0 else 0.0, ALU.mult, ALU.add)\
                                .then_inc(S("tapped_g"), 1)
                            pool.wait_ge(S("tapped_g"), k + 1)
                            z = zz[:, n, 0:SEQ]
                            if w == 0:
                                ins = pool.tensor_copy(z, gtap[:, k % 2, :])
                            else:
                                pool.wait_ge(S("tap_g"), k)
                                ins = TTp(z, z, gtap[:, k % 2, :], ALU.add)
                            ins.then_inc(S("tap_g"), 1)


def _blocks(w):
    k, n = w.shape
    return w.reshape(k // 128, 128, n // 128, 128).transpose(2, 1, 0, 3)


def _rows(v):
    return v.reshape(-1, 128).T


def _cols(w):
    n = w.shape[1] // 512
    return w.reshape(2, 4, 128, n, 512).transpose(3, 0, 2, 1, 4).reshape(2 * n, 128, 4 * 512)


def _layout(np, a):
    f = {k: np.asarray(v) for k, v in a.items()}
    arr = {}
    arr["ada"] = np.concatenate([_cols(f["ada_w"][0]), _cols(f["ada_w"][1]), _cols(f["final_ada_w"])])
    pair = lambda w: _blocks(w).reshape(-1, 2, 128, w.shape[0]).transpose(0, 2, 1, 3).reshape(-1, 128, 2 * w.shape[0])
    arr["rkv"] = np.concatenate([pair(f["rw_wk"][0]), pair(f["rw_wr"][0]), pair(f["rw_wv"][0])])
    arr["wo"] = pair(f["rw_wo"][0])
    arr["pw2"] = pair(f["cv_pw2_w"][0])
    arr["g2"] = f["rw_g2"][0]
    both = lambda u, v: np.concatenate([_blocks(u).reshape(-1, 128, u.shape[0]), _blocks(v).reshape(-1, 128, v.shape[0])], 2)
    arr["up"] = both(f["ffn_w1"][0], f["ffn_w3"][0])
    arr["pw1"] = both(f["cv_pw1_w"][0][:, :D], f["cv_pw1_w"][0][:, D:])
    w2 = _blocks(f["ffn_w2"][0])
    arr["down"] = w2.reshape(NB, 128, 2, FE * 128).transpose(0, 2, 1, 3).reshape(2 * NB, 128, FE * 128)
    arr["moe"] = np.concatenate([
        np.concatenate([both(f["moe_w1"][0, e], f["moe_w3"][0, e]), f["moe_w2"][0, e].reshape(FE, 128, D)], 2)
        for e in range(NE)])
    lo = np.concatenate([f["rw_w1"][0], f["rw_a1"][0], f["rw_g1"][0]], 1)
    arr["lo1"] = lo.reshape(NB, 128, 256).transpose(1, 0, 2)
    arr["lo2"] = np.concatenate([f["rw_w2"][0], f["rw_a2"][0]])
    arr["rw"] = f["moe_router_w"][0].reshape(NB, 128, NE).transpose(1, 0, 2)
    arr["rb"] = f["moe_router_b"]
    dw = f["cv_dw_w"][0].reshape(CW, NB, 128).transpose(2, 1, 0).reshape(128, NB * CW)
    arr["par"] = np.concatenate([_rows(f[k]) for k in (
        "ada_b", "final_ada_b", "norm_mix_g", "norm_ffn_g", "rw_mu", "rw_w0", "rw_a0", "rw_kk", "rw_ka", "rw_rk",
        "rw_lnx_g", "rw_lnx_b", "cv_pw1_b", "cv_dw_b", "cv_ln_g", "cv_ln_b", "cv_pw2_b", "final_g")] + [dw], 1)
    feat = lambda v: v.reshape(-1, NB, 128).transpose(2, 1, 0)
    arr["x"] = feat(np.concatenate([f["x_prompt"][0], f["x_sample"][:, 0]]))
    arr["c"] = feat(np.concatenate([f["c_prompt"], f["c_sample"]]))
    arr["shift"] = feat(f["state_shift"][0])
    arr["conv"] = f["state_conv"][0].reshape(NS, CW - 1, NB, 128).transpose(3, 2, 0, 1).reshape(128, NB * NS, CW - 1)
    arr["state"] = f["state_wkv"][0].reshape(NS, NB, 2, C, C).transpose(1, 2, 4, 0, 3).reshape(NB, 128, NS, C)
    return {k: np.ascontiguousarray(v) for k, v in arr.items()}


_OUTS = {"y": (128, NB, T), "shift_out": (128, NB, NC), "wkv_out": (128, NB, C), "state_out": (NB, 128, NS, C),
         "convp": (128, NB, CW - 1), "convs": (128, NB * NS, CW - 1)}


def kernel(**inputs):
    import numpy as np
    import concourse.bacc as bacc
    from concourse.bass_utils import run_bass_kernel_spmd

    arrays = _layout(np, inputs)
    nc = bacc.Bacc("TRN2", target_bir_lowering=False, num_devices=1)
    io = {k: nc.dram_tensor("in_" + k, a.shape, mybir.dt.from_np(a.dtype), kind="ExternalInput").ap()
          for k, a in arrays.items()}
    io.update({k: nc.dram_tensor("out_" + k, s, F32, kind="ExternalOutput").ap() for k, s in _OUTS.items()})
    build(nc, io)
    got = run_bass_kernel_spmd(nc, [{"in_" + k: a for k, a in arrays.items()}], core_ids=[0]).results[0]
    r = {k: got["out_" + k] for k in _OUTS}
    y = r["y"].transpose(2, 1, 0).reshape(T, D)
    sh = r["shift_out"].transpose(2, 1, 0).reshape(NC, D)
    wkv = r["wkv_out"].reshape(2, C, NB, C).transpose(2, 0, 3, 1).reshape(1, 1, 2 * NB, C, C)
    wkv_s = r["state_out"].reshape(NB, 2, C, NS, C).transpose(3, 0, 1, 4, 2).reshape(1, NS, 2 * NB, C, C)
    cp = r["convp"].transpose(2, 1, 0).reshape(1, 1, CW - 1, D)
    cs = r["convs"].reshape(128, NB, NS, CW - 1).transpose(2, 3, 1, 0).reshape(1, NS, CW - 1, D)
    out = (y[None, :SEQ], y[SEQ:, None], wkv, sh[None, :1], cp, wkv_s, sh[None, 1:], cs)
    return tuple(np.ascontiguousarray(v) for v in out)
```
